# Optimizing a Trainium2 kernel written in Bass

```python
import jax, jax.numpy as jnp
from jax import lax
import numpy as np

D_MODEL = 1024
BATCH = 1
SEQ = 128
DEPTH = 2
DEC_BATCH = 1
DEC_SEQ = 512
PAST_LEN = 128

GRID_W = 64
N_HEADS = 8
N_KV_HEADS = 2
HEAD_DIM = 64
ROPE_AXIS_DIM = HEAD_DIM // 2
ROPE_THETA = 10000.0
Q_BLOCK = 128
D_ATTN = N_HEADS * HEAD_DIM
D_KV = N_KV_HEADS * HEAD_DIM
CHUNK = 128
N_SGU_GROUPS = 4
SGU_GROUP_DIM = 64
D_SGU = N_SGU_GROUPS * SGU_GROUP_DIM
CONV_WIDTH = 3
N_CONV_GROUPS = 4
D_CONV = 256
D_MIX = D_ATTN + D_SGU + D_CONV
D_IN = D_ATTN + 2 * D_KV + 2 * D_SGU + 3 * D_CONV
N_EXPERT_GROUPS = 4
EXPERTS_PER_GROUP = 4
N_EXPERTS = N_EXPERT_GROUPS * EXPERTS_PER_GROUP
TOP_K_IN_GROUP = 2
D_EXPERT = 256
EPS = 1e-6

kernel_name = 'hybrid_diffusion_parallel_heads_step'

def rms_norm(x, g):
    xf = x.astype(jnp.float32)
    y = xf * lax.rsqrt(jnp.mean(xf * xf, axis=-1, keepdims=True) + EPS)
    return (y * g.astype(jnp.float32)).astype(x.dtype)

def axial_rope_tables(n):
    rows = n // GRID_W
    row = jnp.repeat(jnp.arange(rows, dtype=jnp.float32), GRID_W)
    col = jnp.tile(jnp.arange(GRID_W, dtype=jnp.float32), rows)
    half = ROPE_AXIS_DIM // 2
    inv_freq = 1.0 / (ROPE_THETA ** (jnp.arange(half, dtype=jnp.float32) * 2.0 / ROPE_AXIS_DIM))
    ang = jnp.stack([row[:, None] * inv_freq, col[:, None] * inv_freq], axis=1)
    return jnp.cos(ang), jnp.sin(ang)

def apply_axial_rope(x, cos, sin):
    B, n, H, Dh = x.shape
    xf = x.astype(jnp.float32).reshape(B, n, H, 2, 2, ROPE_AXIS_DIM // 2)
    a = xf[..., 0, :]
    b = xf[..., 1, :]
    cs = cos[None, :, None]
    sn = sin[None, :, None]
    out = jnp.stack([a * cs - b * sn, b * cs + a * sn], axis=-2)
    return out.reshape(B, n, H, Dh).astype(x.dtype)

def block_attention(q, k, v):
    B, L, H, Dh = q.shape
    KV = k.shape[2]
    G = H // KV
    nb = L // Q_BLOCK
    qb = jnp.moveaxis(q.reshape(B, nb, Q_BLOCK, KV, G, Dh), 1, 0)
    scale = Dh ** -0.5

    def one_block(qblk):
        s = jnp.einsum('bqkgd,bmkd->bkgqm', qblk, k).astype(jnp.float32) * scale
        p = jax.nn.softmax(s, axis=-1).astype(v.dtype)
        return jnp.einsum('bkgqm,bmkd->bqkgd', p, v)

    o = lax.map(one_block, qb)
    return jnp.moveaxis(o, 0, 1).reshape(B, L, H * Dh)

def chunk_sgu(u, v, w_s, b_s):
    B, L, C = v.shape
    nc = L // CHUNK
    vr = v.reshape(B, nc, CHUNK, N_SGU_GROUPS, SGU_GROUP_DIM)
    mixed = jnp.einsum('gpq,bnqgc->bnpgc', w_s, vr) + jnp.transpose(b_s)[:, :, None]
    return u * mixed.reshape(B, L, C)

def short_gated_conv(bg, cg, xs, w):
    z = cg * xs
    zp = jnp.pad(z, ((0, 0), (1, 1), (0, 0)))
    conv = zp[:, :-2] * w[0] + zp[:, 1:-1] * w[1] + zp[:, 2:] * w[2]
    return bg * conv

def hierarchical_moe(h, rg_w, rg_b, re_w, re_b, w1, w3, w2):
    B, L, D = h.shape
    t = h.reshape(B * L, D)
    g_logits = (t @ rg_w + rg_b).astype(jnp.float32)
    g_prob = jax.nn.softmax(g_logits, axis=-1)
    g_idx = jnp.argmax(g_logits, axis=-1)
    p_g = jnp.take_along_axis(g_prob, g_idx[:, None], axis=-1)
    e_all = jnp.einsum('td,gde->tge', t, re_w) + re_b
    e_logits = jnp.take_along_axis(e_all, g_idx[:, None, None], axis=1)[:, 0].astype(jnp.float32)
    e_prob = jax.nn.softmax(e_logits, axis=-1)
    top_v, top_i = lax.top_k(e_prob, TOP_K_IN_GROUP)
    top_v = top_v / jnp.sum(top_v, axis=-1, keepdims=True)
    expert_id = g_idx[:, None] * EXPERTS_PER_GROUP + top_i
    weight = (p_g * top_v).astype(t.dtype)
    gates = jnp.sum(jax.nn.one_hot(expert_id, N_EXPERTS, dtype=t.dtype) * weight[..., None], axis=1)
    hid = jax.nn.silu(jnp.einsum('td,edf->tef', t, w1)) * jnp.einsum('td,edf->tef', t, w3)
    out = jnp.einsum('tef,efd->td', hid * gates[:, :, None], w2)
    return out.reshape(B, L, D)

def trunk_layer(x, mod, p, rope, ctx_kv):
    B, L, _ = x.shape
    shift1, scale1, gate1, shift2, scale2, gate2 = jnp.split(mod[:, None, :], 6, axis=-1)
    h = rms_norm(x, p['norm1']) * (1.0 + scale1) + shift1
    proj = h @ p['w_in']
    sizes = (D_ATTN, D_KV, D_KV, D_SGU, D_SGU, D_CONV, D_CONV, D_CONV)
    offs = [int(o) for o in np.cumsum(sizes)[:-1]]
    q, k, v, su, sv, cb, cc, cx = jnp.split(proj, offs, axis=-1)
    q = rms_norm(q.reshape(B, L, N_HEADS, HEAD_DIM), p['q_norm'])
    k = rms_norm(k.reshape(B, L, N_KV_HEADS, HEAD_DIM), p['k_norm'])
    v = v.reshape(B, L, N_KV_HEADS, HEAD_DIM)
    if rope is not None:
        q = apply_axial_rope(q, rope[0], rope[1])
        k = apply_axial_rope(k, rope[0], rope[1])
    if ctx_kv is not None:
        k_all = jnp.concatenate([k, ctx_kv[0]], axis=1)
        v_all = jnp.concatenate([v, ctx_kv[1]], axis=1)
    else:
        k_all, v_all = k, v
    attn = block_attention(q, k_all, v_all)
    sgu = chunk_sgu(su, sv, p['sgu_w'], p['sgu_b'])
    conv = short_gated_conv(cb, cc, cx, p['conv_w'])
    on = p['out_norm']
    merged = jnp.concatenate([
        rms_norm(attn, on[:D_ATTN]),
        rms_norm(sgu, on[D_ATTN:D_ATTN + D_SGU]),
        rms_norm(conv, on[D_ATTN + D_SGU:]),
    ], axis=-1)
    x = x + gate1 * (merged @ p['w_out'])
    h2 = rms_norm(x, p['norm2']) * (1.0 + scale2) + shift2
    x = x + gate2 * hierarchical_moe(h2, p['router_g_w'], p['router_g_b'], p['router_e_w'],
                                     p['router_e_b'], p['moe_w1'], p['moe_w3'], p['moe_w2'])
    return x, k, v

def setup_inputs(seed: int = 0) -> dict:
    key = jax.random.key(seed)
    ks = jax.random.split(key, 32)
    f32 = jnp.float32

    def nrm(k, shape, scale):
        return jax.random.normal(k, shape, f32) * scale

    def gain(k, shape):
        return 1.0 + 0.02 * jax.random.normal(k, shape, f32)

    D = D_MODEL
    return {
        'x_prompt': nrm(ks[0], (BATCH, SEQ, D), 1.0),
        'x_sample': nrm(ks[1], (DEC_BATCH, DEC_SEQ, D), 1.0),
        'cache_k': nrm(ks[2], (DEC_BATCH, DEPTH, PAST_LEN, N_KV_HEADS, HEAD_DIM), 1.0),
        'cache_v': nrm(ks[3], (DEC_BATCH, DEPTH, PAST_LEN, N_KV_HEADS, HEAD_DIM), 0.5),
        'c': nrm(ks[4], (DEC_BATCH, D), 1.0),
        'c_ctx': nrm(ks[5], (D,), 1.0),
        'w_ada': nrm(ks[6], (DEPTH, D, 6 * D), 0.5 * D ** -0.5),
        'b_ada': nrm(ks[7], (DEPTH, 6 * D), 0.02),
        'norm1': gain(ks[8], (DEPTH, D)),
        'w_in': nrm(ks[9], (DEPTH, D, D_IN), D ** -0.5),
        'q_norm': gain(ks[10], (DEPTH, HEAD_DIM)),
        'k_norm': gain(ks[11], (DEPTH, HEAD_DIM)),
        'sgu_w': nrm(ks[12], (DEPTH, N_SGU_GROUPS, CHUNK, CHUNK), CHUNK ** -0.5),
        'sgu_b': gain(ks[13], (DEPTH, N_SGU_GROUPS, CHUNK)),
        'conv_w': nrm(ks[14], (DEPTH, CONV_WIDTH, D_CONV), CONV_WIDTH ** -0.5),
        'out_norm': gain(ks[15], (DEPTH, D_MIX)),
        'w_out': nrm(ks[16], (DEPTH, D_MIX, D), D_MIX ** -0.5),
        'norm2': gain(ks[17], (DEPTH, D)),
        'router_g_w': nrm(ks[18], (DEPTH, D, N_EXPERT_GROUPS), D ** -0.5),
        'router_g_b': nrm(ks[19], (DEPTH, N_EXPERT_GROUPS), 0.01),
        'router_e_w': nrm(ks[20], (DEPTH, N_EXPERT_GROUPS, D, EXPERTS_PER_GROUP), D ** -0.5),
        'router_e_b': nrm(ks[21], (DEPTH, N_EXPERT_GROUPS, EXPERTS_PER_GROUP), 0.01),
        'moe_w1': nrm(ks[22], (DEPTH, N_EXPERTS, D, D_EXPERT), D ** -0.5),
        'moe_w3': nrm(ks[23], (DEPTH, N_EXPERTS, D, D_EXPERT), D ** -0.5),
        'moe_w2': nrm(ks[24], (DEPTH, N_EXPERTS, D_EXPERT, D), D_EXPERT ** -0.5),
        'final_norm': gain(ks[25], (D,)),
    }

def reference(x_prompt, x_sample, cache_k, cache_v, c, c_ctx, w_ada, b_ada, norm1, w_in,
              q_norm, k_norm, sgu_w, sgu_b, conv_w, out_norm, w_out, norm2, router_g_w,
              router_g_b, router_e_w, router_e_b, moe_w1, moe_w3, moe_w2, final_norm):
    def layer_params(l):
        return dict(norm1=norm1[l], w_in=w_in[l], q_norm=q_norm[l], k_norm=k_norm[l],
                    sgu_w=sgu_w[l], sgu_b=sgu_b[l], conv_w=conv_w[l], out_norm=out_norm[l],
                    w_out=w_out[l], norm2=norm2[l], router_g_w=router_g_w[l],
                    router_g_b=router_g_b[l], router_e_w=router_e_w[l], router_e_b=router_e_b[l],
                    moe_w1=moe_w1[l], moe_w3=moe_w3[l], moe_w2=moe_w2[l])

    xp = x_prompt
    ctx_ks = []
    ctx_vs = []
    for l in range(DEPTH):
        mod_ctx = jax.nn.silu(c_ctx)[None, :] @ w_ada[l] + b_ada[l]
        xp, k_l, v_l = trunk_layer(xp, mod_ctx, layer_params(l), None, None)
        ctx_ks.append(k_l)
        ctx_vs.append(v_l)
    y_prompt = rms_norm(xp, final_norm)
    new_cache_k = jnp.stack(ctx_ks, axis=1)
    new_cache_v = jnp.stack(ctx_vs, axis=1)

    cos, sin = axial_rope_tables(x_sample.shape[1])
    xs = x_sample
    for l in range(DEPTH):
        mod_lat = jax.nn.silu(c) @ w_ada[l] + b_ada[l]
        xs, _, _ = trunk_layer(xs, mod_lat, layer_params(l), (cos, sin),
                               (cache_k[:, l], cache_v[:, l]))
    y_sample = rms_norm(xs, final_norm)

    return (y_prompt, y_sample, new_cache_k, new_cache_v)


_drawn_inputs = setup_inputs


def setup_inputs(seed=0):
    import zlib

    import numpy as np

    out = dict(_drawn_inputs(seed))
    spreads = {}
    factors = {'cache_k': 3.337,
     'cache_v': 2.776,
     'norm1': 2.748,
     'q_norm': 8.0,
     'sgu_b': 8.0,
     'out_norm': 3.333,
     'norm2': 4.001,
     'router_g_b': 7.496,
     'router_e_b': 8.0,
     'final_norm': 2.801}
    for name, (base, spread) in spreads.items():
        noise = np.random.default_rng([zlib.crc32(name.encode()), seed]).standard_normal(out[name].shape)
        drawn = base * np.exp(spread * noise) if base else spread * noise
        out[name] = __import__('jax').numpy.asarray(drawn.astype(out[name].dtype))
    for name, factor in factors.items():
        out[name] = (out[name] * factor).astype(out[name].dtype)
    return out
```

```python
from contextlib import ExitStack

import concourse.bass as bass
from concourse import mybir

P = 128
D = 1024
DEPTH = 2
NT = 5
NLT = 4
CTX = 4
TOK = NT * P
KD = D // P
NH, NKV, HD = 8, 2, 64
D_IN = 2048
NG, NE, EPG = 4, 16, 4
F = 256
EPS = 1e-6
U = 2048
N = 512
RAWS = 4
HLS = 3
PAIRS = 2 * TOK
MINB = PAIRS // P
MAXB = PAIRS // P + NE - 1
LB = MAXB + 1
NOROW = 8192
CACHE, CTXK = 4, 5
NKEY = 6

F32 = mybir.dt.float32
F32R = mybir.dt.float32r
BF16 = mybir.dt.bfloat16
I32 = mybir.dt.int32
U32 = mybir.dt.uint32
ALU = mybir.AluOpType
ACT = mybir.ActivationFunctionType
X = mybir.AxisListType.X

UNITS = ([("ada", i) for i in range(24)] + [("w", i) for i in range(8)] + [("w", i) for i in range(8, 12)])
NU = len(UNITS)


PER_LAYER = {
    "ada_read": 24, "piece_done": 12, "piece_out0": 96, "piece_out1": 96, "bias_in0": 96, "bias_in1": 96,
    "norm2_in": 32, "params_loaded": 17 * 16, "tabs": 6, "modc_part": 3, "modc_psum": 1, "a1_ready": 1,
    "ss1": NT, "rstd1": 1, "xr_ready": NT, "hT_psum": KD, "h_full": 2 * KD, "h_hi": KD, "h_lo": KD,
    "w_hi": 12, "w_lo": 12, "w_used": 6, "proj": 4 * NT, "proj_read": 4 * NT, "zpn_zero": 2,
    "sq": 2 * NT, "ssqk": 2 * NT, "rqk": 2 * NT, "kv_raw": NT, "sv_raw": NT, "q_final": NT, "k_final": NT,
    "z_done": NT, "shifted": 64, "tap2": 1, "conv_done": 1, "sgT_psum": 1, "sgT_ready": 1, "sgu_psum": 4, "sgu_done": 4,
    "v_hi": NKV, "v_lo": NKV, "k_hi": NKEY, "k_lo": NKEY, "kT_psum": NKEY, "kk": NKEY,
    "q_hi": NT, "q_lo": NT, "qT_psum": 2 * NT, "qT": 2 * NT, "scores": NT * NH, "nmax": NT * NH, "prob": NT * NH,
    "pT_psum": NT * NH, "pT_hi": NT * NH, "pT_lo": NT * NH, "pv": NT * NH, "o_low": 2 * NT, "o_read": 2 * NT,
    "attn_done": 2 * NT, "ss3": 3 * NT, "rstd3": 1, "mrg_ready": 3 * NT, "mT_psum": KD, "mT_hi": 2 * KD, "mT_lo": 2 * KD,
    "gate1_row": 32, "scale2_row": 32, "shift2_row": 32, "gate2_row": 32, "oproj_psum": 2 * NT, "oproj": 2 * NT,
    "x_attn": 2 * NT, "ss2": NT, "rstd2": NT, "h2": NT, "h2T_psum": NT, "h2T": NT, "h2_stored0": 48, "h2_stored1": 32, "logits": NT,
    "rt_exp_in": 2, "rt_exp": 2, "choice": 1, "counts_psum": 1, "lists": 1, "list_psum": 1, "xg_zero": 1, "ctl_ready": 1,
    "y_read": 2 * NT, "y_in0": 16 * NT, "y_in1": 16 * NT, "moe_split_done": 1, "x_moe": NT,
}


def f32(ap):
    return ap.bitcast(F32)


def build(nc, I, O):
    with ExitStack() as ctx:
        def sb(name, shape, dt=F32):
            return ctx.enter_context(nc.sbuf_tensor(name, shape, dt))

        sems = {}

        def sem(name):
            if name not in sems:
                sems[name] = ctx.enter_context(nc.semaphore(name))
            return sems[name]

        modrow = [nc.dram_tensor(f"modrow{l}", [2, 6 * D], F32, kind="Internal").ap() for l in range(DEPTH)]
        h2s = [nc.dram_tensor(f"h2s{l}", [TOK, D], F32, kind="Internal").ap() for l in range(DEPTH)]
        ys = nc.dram_tensor("ys", [MAXB * P, D], F32, kind="Internal").ap()

        x = sb("x", [P, NT, D])
        actH = sb("actH", [P, KD * TOK], F32R)
        actL = sb("actL", [P, KD * TOK], F32R)
        raw = sb("raw", [P, RAWS, U])
        wH = sb("wH", [P, HLS, U], F32R)
        wL = sb("wL", [P, HLS, U], F32R)
        pool = sb("pool", [P, 13312])
        ident = sb("ident", [P, P])
        iota = sb("iota", [P, P])
        ones = sb("ones", [P, P], BF16)
        upper = sb("upper", [P, P], BF16)
        tabs = sb("tabs", [P, NT, 2, 2, HD])
        cw = sb("cw", [P, 3, 256])
        sgw = sb("sgw", [P, 4, P])
        sgb = sb("sgb", [P, 4])
        rw = sb("rw", [P, KD, NG + NE])
        rb = sb("rb", [P, NG + NE])
        gains = sb("gains", [P, 2, HD])
        cols = sb("cols", [P, 2 * KD])
        csil = sb("csil", [P, KD, 2])
        modc = sb("modc", [P, 16, 2])
        stat = sb("stat", [P, 64])
        nhalf = sb("nhalf", [P, 16])
        rsum = sb("rsum", [P, 2 * NH])
        nmax = sb("nmax", [P, 4])
        rinv = sb("rinv", [P, NH])
        pcon = sb("pcon", [P, 64])
        gate = sb("gate", [P, 2, NT])
        slot = sb("slot", [P, 2 * NT], U32)
        idxs = sb("idxs", [P, LB], U32)
        idxc = sb("idxc", [P, 1], U32)
        ctl = sb("ctl", [1, 32], I32)
        ps = ctx.enter_context(nc.psum_tensor("ps", [P, 8, 512], F32))

        actHk = actH[:, :].rearrange("p (k t) -> p k t", k=KD)
        actLk = actL[:, :].rearrange("p (k t) -> p k t", k=KD)
        kk = actH[:, 0:3072].rearrange("p (c n) -> p c n", c=4)
        pTH = actH[:, 3072:4352].rearrange("p (b n) -> p b n", b=2)
        pTL = actL[:, 3072:4352].rearrange("p (b n) -> p b n", b=2)
        vv = [t[:, 4352:5120].rearrange("p (j n) -> p j n", j=NKEY) for t in (actH, actL)]
        qT = actL[:, 0:2048].rearrange("p (b h n) -> p b h n", b=2, h=NH)
        qhl = actL[:, 2048:3072].rearrange("p (h s d) -> p h s d", h=NH, s=2)
        kdup = actL[:, 2048:3072].rearrange("p (b v s d) -> p b v s d", b=2, v=NKV, s=4)
        xTH = actH[:, 0:1024].rearrange("p (k n) -> p k n", k=KD)
        xTL = actL[:, 0:1024].rearrange("p (k n) -> p k n", k=KD)
        hTH = actH[:, 1024:1280].rearrange("p (k n) -> p k n", k=2)
        hTL = actL[:, 1024:1280].rearrange("p (k n) -> p k n", k=2)

        mrg = pool[:, 0:5120].rearrange("p (t n) -> p t n", t=NT)
        aux = pool[:, 5120:10240]
        pbuf = pool[:, 10240:11776]
        kv = pool[:, 11776:13312].rearrange("p (j n) -> p j n", j=NKEY)
        piece = pool[0:2, 0:1024].rearrange("p (b n) -> p b n", b=2)
        bpiece = pool[0:2, 1024:2048].rearrange("p (b n) -> p b n", b=2)
        npiece = pool[0:2, 2048:3072].rearrange("p (b n) -> p b n", b=2)
        rtab = pool[:, 3072:3712].rearrange("p (t c d) -> p t c d", t=NT, c=2)
        junk1 = pool[:, 3712:4736]
        xr = aux.rearrange("p (t n) -> p t n", t=NT)
        hf = pbuf[:, 0:1280].rearrange("p (b n) -> p b n", b=2)
        sv = aux[:, 0:1280].rearrange("p (t n) -> p t n", t=NT)
        z = aux[:, 1280:2560].rearrange("p (t n) -> p t n", t=NT)
        zp = aux[:, 2560:3840].rearrange("p (t n) -> p t n", t=NT)
        zn = aux[:, 3840:5120].rearrange("p (t n) -> p t n", t=NT)
        sgT = pbuf[:, 1024:1536].rearrange("p (g q) -> p g q", g=4)
        prob = pbuf[:, 0:1280].rearrange("p (b n) -> p b n", b=2)
        grow = aux[:, 0:2048].rearrange("p (c n) -> p c n", c=2)
        arow = aux[:, 2048:4096].rearrange("p (c n) -> p c n", c=2)
        h2T = aux[:, 4096:5120].rearrange("p (k n) -> p k n", k=KD)
        srow = pool[:, 0:2048].rearrange("p (c n) -> p c n", c=2)
        h2b = pool[:, 2048:4096].rearrange("p (b n) -> p b n", b=2)
        otmp = pool[:, 2048:4096].rearrange("p (b n) -> p b n", b=4)
        frow = pool[:, 4096:5120]
        xg = pool[:, 10240:11264]
        hid = pool[:, 11264:11776]
        yb = pool[:, 11776:12800]
        rt = pool[:, 11264:13312]
        used = [0]

        def tmp(*shape, dt=F32):
            n = 1
            for s_ in shape:
                n *= s_
            if dt == BF16:
                n //= 2
            v = rt[:, used[0]:used[0] + n]
            used[0] += n
            v = v if dt == F32 else v.bitcast(dt)
            names = " ".join("abcd"[:len(shape)])
            return v if len(shape) == 1 else v.rearrange(f"p ({names}) -> p {names}", **dict(zip("abcd", shape)))

        pr2 = tmp(160)
        ex, d_ = tmp(NT, 4), tmp(NT)
        lg, gm, sm, eq = tmp(NT, NG + NE), tmp(NT), tmp(NT), tmp(NT, 4)
        og, o1, o2, es, e2 = (tmp(NT, 4) for _ in range(5))
        em1, em2, pg = tmp(NT), tmp(NT), tmp(NT)
        pr = tmp(NT, 4, 4)
        M = tmp(2, NT, NE)
        Mb = tmp(NT, NE, dt=BF16)
        pos, cnt, cmp5 = tmp(NT * NE), tmp(NE), tmp(NE, 5)
        nb_, incl, base = tmp(NE), tmp(NE), tmp(NE)
        q, eb, qd = tmp(10), tmp(10), tmp(10)
        oneb = tmp(10, LB, dt=BF16)
        tl = tmp(10, 2, LB, dt=BF16)
        eb26 = tmp(32)
        one_r = pool[:, 10240:10880].bitcast(BF16).rearrange("p (c n) -> p c n", c=10)

        s_raw = [sem(f"raw_loaded{i}") for i in range(RAWS)]
        block = ctx.enter_context(nc.Block())

        def S(name, l):
            return sem(f"{name}_{l}")

        def at(name, l, n):
            return l * PER_LAYER[name] + n

        def unit_used(eng, l, i):
            kind, n = UNITS[i]
            if kind == "ada":
                eng.wait_ge(sem("ada_read"), at("ada_read", l, n + 1))
            else:
                eng.wait_ge(sem("w_lo"), at("w_lo", l, n + 1))

        def unit_loaded(eng, l, i):
            eng.wait_ge(s_raw[i % RAWS], 16 * (l * (NU // RAWS) + i // RAWS + 1))

        units = {u: i for i, u in enumerate(UNITS)}

        def w_read(eng, l, i):
            if i % 2 == 0:
                eng.wait_ge(sem("w_used"), at("w_used", l, i // 2 + 1))
            elif i < 8:
                eng.wait_ge(sem("proj"), at("proj", l, NT * (i // 2 + 1)))
            else:
                eng.wait_ge(sem("oproj_psum"), at("oproj_psum", l, NT * (i // 2 - 3)))

        @block.sync
        def _(sp):
            sp.dma_start(csil[:, :, 0], I["c"].rearrange("a (k p) -> p (a k)", p=P),
                         allow_slow_non_contiguous=True).then_inc(sem("c_loaded"), 16)
            sp.dma_start(csil[:, :, 1], I["c_ctx"].rearrange("(k p) -> p k", p=P),
                         allow_slow_non_contiguous=True).then_inc(sem("c_loaded"), 16)
            for l in range(DEPTH):
                for i, (kind, n) in enumerate(UNITS):
                    if i >= RAWS:
                        unit_used(sp, l, i - RAWS)
                    elif l > 0 and i < HLS:
                        sp.wait_ge(sem("moe_split_done"), at("moe_split_done", l - 1, 1))
                    elif l > 0:
                        unit_used(sp, l - 1, NU - RAWS + i)
                    if l == 0 and i == 8:
                        sp.dma_start(x[:, 0:NLT, :], I["x_sample"].rearrange("a (t p) d -> p (a t) d", p=P)
                                     ).then_inc(sem("x_loaded"), 16)
                        sp.dma_start(x[:, CTX, :], I["x_prompt"].rearrange("a p d -> p (a d)")
                                     ).then_inc(sem("x_loaded"), 16)
                    if l == 0 and i == 32:
                        sp.wait_ge(sem("x_loaded"), 32)
                        for j in range(MINB, MAXB):
                            sp.dma_start(ys[j * P:(j + 1) * P, :], x[:, 0, :]).then_inc(sem("ys_filled"), 16)
                    k0, n0 = (n % 2) * 4, (n // 2) * N
                    if kind == "ada":
                        src = I["w_ada"][l, k0 * P:(k0 + 4) * P, n0:n0 + N]
                    elif n < 8:
                        src = I["w_in"][l, k0 * P:(k0 + 4) * P, n0:n0 + N]
                    else:
                        n0 -= 4 * N
                        src = I["w_out"][l, k0 * P:(k0 + 4) * P, n0:n0 + N]
                    sp.dma_start(raw[:, i % RAWS, :].rearrange("p (k n) -> p k n", k=4),
                                 src.rearrange("(k p) n -> p k n", p=P)).then_inc(s_raw[i % RAWS], 16)

                w1, w3, w2 = I["moe_w1"][l], I["moe_w3"][l], I["moe_w2"][l]

                def load_expert(e, slot_free=None):
                    for u in range(2):
                        if slot_free is not None:
                            sp.wait_ge(S("m_lo", l), slot_free + u)
                        for j, w in enumerate((w1, w3)):
                            sp.dma_start(
                                raw[:, u, :].rearrange("p (k j f) -> p k j f", k=4, j=2)[:, :, j, :],
                                w[bass.ds(e, 1), u * N:(u + 1) * N, :].rearrange("a (k p) f -> p (a k) f", p=P)
                            ).then_inc(S(f"m_raw{u}", l), 16)
                    if slot_free is not None:
                        sp.wait_ge(S("m_lo", l), slot_free + 2)
                    sp.dma_start(raw[:, 2, :].rearrange("p (k n) -> p k n", k=2),
                                 w2[bass.ds(e, 1), :, :].rearrange("a (k p) n -> p (a k) n", p=P)
                                 ).then_inc(S("m_raw2", l), 16)

                def store_block(b):
                    sp.wait_ge(S("m_ya", l), b + 2)
                    sp.wait_ge(S("m_yd", l), b + 2)
                    sp.dma_start(ys[bass.ds(b * P, P), :], yb[:, :]).then_inc(S("m_ys", l), 16)

                sp.wait_ge(sem("ctl_ready"), at("ctl_ready", l, 1))
                if l == 0:
                    sp.wait_ge(sem("ys_filled"), 16 * (MAXB - MINB))
                last = sp.value_load(ctl[0:1, 0:1], min_val=1, max_val=MAXB - 1)
                e0 = sp.value_load(ctl[0:1, 1:2], min_val=0, max_val=NE - 1)
                for i in range(NU - RAWS, NU - 1):
                    unit_used(sp, l, i)
                load_expert(e0)
                with sp.Fori(0, last) as b:
                    e = sp.value_load(ctl[0:1, bass.ds(b + 2, 1)], min_val=0, max_val=NE - 1)
                    load_expert(e, 3 * b + 1)
                    store_block(b)
                store_block(last)

        @block.gpsimd
        def _(pl):
            pl.dma_start(ident[:, :], I["k_ident"]).then_inc(sem("ident_loaded"), 16)
            pl.dma_start(iota[:, :], I["k_iota"]).then_inc(sem("consts_loaded"), 16)
            pl.dma_start(pcon[:, :], I["k_pcon"]).then_inc(sem("consts_loaded"), 16)
            pl.dma_start(rt[:, 0:P], I["k_upper"]).then_inc(sem("consts_loaded"), 16)
            pl.memset(nhalf[:, :], -0.5).then_inc(sem("nhalf_set"), 1)
            pl.wait_ge(sem("nhalf_set"), 1)
            steps = [0]

            def link(ins):
                steps[0] += 1
                ins.then_inc(sem("pool_step"), 1)
                pl.wait_ge(sem("pool_step"), steps[0])

            def rstd(src, dst, n, width, ready, count, done):
                pl.wait_ge(ready, count)
                link(pl.tensor_scalar(dst, src, 1.0 / width, EPS, ALU.mult, ALU.add))
                pl.tensor_tensor(dst, dst, nhalf[:, 0:n], ALU.pow).then_inc(done, 1)

            def row(ap):
                return ap.partition_broadcast(P)

            for l in range(DEPTH):
                if l > 0:
                    pl.wait_ge(sem("x_moe"), at("x_moe", l - 1, NT))
                lp = sem("params_loaded")
                pl.dma_start(rtab, I["k_rope"]).then_inc(lp, 16)
                pl.dma_start(gains[:, 0, :], row(I["q_norm"][l])).then_inc(lp, 16)
                pl.dma_start(gains[:, 1, :], row(I["k_norm"][l])).then_inc(lp, 16)
                pl.dma_start(cols[:, 0:KD], I["norm1"][l].rearrange("(k p) -> p k", p=P),
                             allow_slow_non_contiguous=True).then_inc(lp, 16)
                pl.dma_start(cols[:, KD:], I["out_norm"][l].rearrange("(k p) -> p k", p=P),
                             allow_slow_non_contiguous=True).then_inc(lp, 16)
                pl.dma_start(cw[:, :, :].rearrange("p w n -> p (w n)"), row(I["conv_w"][l].rearrange("w n -> (w n)"))).then_inc(lp, 16)
                pl.dma_start(sgw[:, :, :], I["sgu_w"][l].rearrange("g p q -> p g q")).then_inc(lp, 16)
                pl.dma_start(sgb[:, :], I["sgu_b"][l].rearrange("g p -> p g"),
                             allow_slow_non_contiguous=True).then_inc(lp, 16)
                pl.dma_start(rw[:, :, 0:NG], I["router_g_w"][l].rearrange("(k p) g -> p k g", p=P)).then_inc(lp, 16)
                for g in range(NG):
                    pl.dma_start(rw[:, :, NG + EPG * g:NG + EPG * (g + 1)],
                                 I["router_e_w"][l, g].rearrange("(k p) e -> p k e", p=P)).then_inc(lp, 16)
                pl.dma_start(rb[:, 0:NG], row(I["router_g_b"][l])).then_inc(lp, 16)
                pl.dma_start(rb[:, NG:], row(I["router_e_b"][l].rearrange("g e -> (g e)"))).then_inc(lp, 16)
                pl.dma_start(kv[:, CACHE, 0:P], I["cache_k"][0, l].rearrange("m h d -> m (h d)")).then_inc(lp, 16)
                pl.dma_start(kv[:, CACHE, P:], I["cache_v"][0, l].rearrange("m h d -> m (h d)")).then_inc(lp, 16)

                def bias_in(g):
                    pl.dma_start(bpiece[:, g % 2, :], I["b_ada"][l, g * N:(g + 1) * N].partition_broadcast(2)
                                 ).then_inc(sem(f"bias_in{g % 2}"), 16)
                for h in range(2):
                    pl.dma_start(npiece[:, h, :], I["norm2"][l, h * N:(h + 1) * N].partition_broadcast(2)
                                 ).then_inc(sem("norm2_in"), 16)
                bias_in(0)
                bias_in(1)
                for g in range(12):
                    if g == 3:
                        rstd(stat[:, 0:NT], stat[:, 8:8 + NT], NT, D, sem("ss1"), at("ss1", l, NT), sem("rstd1"))
                    pl.wait_ge(sem("piece_done"), at("piece_done", l, g + 1))
                    pl.dma_start(modrow[l][:, g * N:(g + 1) * N], piece[:, g % 2, :]).then_inc(sem(f"piece_out{g % 2}"), 16)
                    if g + 2 < 12:
                        bias_in(g + 2)

                pl.wait_ge(sem("hT_psum"), at("hT_psum", l, KD))
                pl.memset(zp[:, :, :], 0.0).then_inc(sem("zpn_zero"), 1)
                pl.memset(zn[:, :, :], 0.0).then_inc(sem("zpn_zero"), 1)
                for i in range(2 * NT):
                    n = NH if i < NT else NKV
                    rstd(stat[:, 16:16 + n], stat[:, 24:24 + n], n, HD, sem("ssqk"), at("ssqk", l, i + 1), sem("rqk"))
                pl.wait_ge(sem("shifted"), at("shifted", l, 64))
                pl.tensor_tensor(zn[:, :, :], zn[:, :, :], cw[:, 2, :].unsqueeze(1).to_broadcast([P, NT, 256]),
                                 ALU.mult).then_inc(sem("tap2"), 1)
                pl.wait_ge(sem("conv_done"), at("conv_done", l, 1))
                pl.wait_ge(sem("sgu_done"), at("sgu_done", l, 4))
                for p_ in range(2):
                    pl.wait_ge(sem(f"piece_out{p_}"), at(f"piece_out{p_}", l, 96))
                for c in range(2):
                    pl.dma_start(grow[:, c, :], row(modrow[l][c, 2 * D:3 * D])).then_inc(sem("gate1_row"), 16)
                    pl.dma_start(arow[:, c, :], row(modrow[l][c, 4 * D:5 * D])).then_inc(sem("scale2_row"), 16)
                pl.wait_ge(sem("ss3"), at("ss3", l, 3 * NT))
                link(pl.tensor_scalar(stat[:, 32:37], stat[:, 32:37], 1.0 / 512, EPS, ALU.mult, ALU.add))
                link(pl.tensor_scalar(stat[:, 37:47], stat[:, 37:47], 1.0 / 256, EPS, ALU.mult, ALU.add))
                pl.tensor_tensor(stat[:, 48:63], stat[:, 32:47], nhalf[:, 0:15], ALU.pow).then_inc(sem("rstd3"), 1)
                pl.wait_ge(sem("mT_psum"), at("mT_psum", l, KD))
                for c in range(2):
                    pl.dma_start(srow[:, c, :], row(modrow[l][c, 3 * D:4 * D])).then_inc(sem("shift2_row"), 16)
                if l == DEPTH - 1:
                    pl.dma_start(frow, row(I["final_norm"])).then_inc(sem("final_row"), 16)
                for i in range(2 * NT):
                    nb, t = divmod(i, NT)
                    xs = x[:, t, nb * N:(nb + 1) * N]
                    pl.wait_ge(sem("oproj"), at("oproj", l, i + 1))
                    pl.tensor_tensor(xs, xs, otmp[:, i % 4, :], ALU.add).then_inc(sem("x_attn"), 1)
                for c in range(2):
                    pl.dma_start(grow[:, c, :], row(modrow[l][c, 5 * D:6 * D])).then_inc(sem("gate2_row"), 16)
                for t in range(NT):
                    rstd(stat[:, t:t + 1], stat[:, 8 + t:9 + t], 1, D, sem("ss2"), at("ss2", l, t + 1), sem("rstd2"))

                pl.wait_ge(sem("xg_zero"), at("xg_zero", l, 1))

                def gather(b):
                    pl.tensor_copy(idxc[:, :], idxs[:, bass.ds(b, 1)]).then_inc(S("m_idx", l), 1)
                    pl.wait_ge(S("m_idx", l), b + 1)
                    pl.sem_inc(sem("pool_passed"), 1)
                    pl.indirect_dma_start(xg, None, h2s[l], bass.IndirectOffsetOnAxis(idxc[:, 0:1], 0),
                                          bounds_check=TOK - 1, oob_is_err=False).then_inc(S("m_g", l), 16)

                pl.wait_ge(sem("ctl_ready"), at("ctl_ready", l, 1))
                for p_ in range(2):
                    pl.wait_ge(sem(f"h2_stored{p_}"), at(f"h2_stored{p_}", l + 1, 0))
                last = pl.value_load(ctl[0:1, 0:1], min_val=1, max_val=MAXB - 1)
                gather(0)
                with pl.Fori(0, last) as b:
                    pl.wait_ge(S("m_tx", l), b + 1)
                    pl.sem_inc(sem("pool_passed"), 1)
                    gather(b + 1)
                pl.wait_ge(S("m_ys", l), (last + 2) * 16)
                pl.sem_inc(sem("pool_passed"), 1)
                for i in range(2 * NT):
                    t, c = divmod(i, 2)
                    if i >= 2:
                        pl.wait_ge(sem("y_read"), at("y_read", l, i - 1))
                    pl.indirect_dma_start(h2b[:, c, :], None, ys,
                                          bass.IndirectOffsetOnAxis(slot[:, c * NT + t:c * NT + t + 1], 0)
                                          ).then_inc(sem(f"y_in{c}"), 16)
            for t in range(NT):
                rstd(stat[:, t:t + 1], stat[:, 8 + t:9 + t], 1, D, sem("ssf"), t + 1, sem("rstdf"))

        @block.scalar
        def _(act):
            steps = [0]

            def link(ins):
                steps[0] += 1
                ins.then_inc(sem("act_step"), 1)
                act.wait_ge(sem("act_step"), steps[0])

            act.wait_ge(sem("c_loaded"), 32)
            act.activation(csil[:, :, :], csil[:, :, :], ACT.Silu).then_inc(sem("c_silu"), 1)
            act.wait_ge(sem("x_loaded"), 32)

            for l in range(DEPTH):
                def split_hi(i):
                    unit_loaded(act, l, units[("w", i)])
                    if i >= HLS:
                        w_read(act, l, i - HLS)
                    act.activation(wH[:, i % HLS, :], raw[:, units[("w", i)] % RAWS, :], ACT.Copy).then_inc(sem("w_hi"), 1)

                for t in range(NT):
                    if t:
                        act.wait_ge(sem("ss1"), at("ss1", l, t))
                    elif l:
                        act.wait_ge(sem("x_moe"), at("x_moe", l - 1, NT))
                    act.activation(junk1, x[:, t, :], ACT.Square, accum_out=stat[:, t:t + 1]).then_inc(sem("ss1"), 1)
                for k in range(KD):
                    act.wait_ge(sem("hT_psum"), at("hT_psum", l, k + 1))
                    if k == 0:
                        act.wait_ge(sem("a1_ready"), at("a1_ready", l, 1))
                    if k >= 2:
                        act.wait_ge(sem("h_lo"), at("h_lo", l, k - 1))
                    b0 = 2 * (k % 2)
                    act.activation(hf[:, k % 2, 0:512], ps[:, b0, :], ACT.Identity,
                                   bias=modc[:, k, 0:1], scale=modc[:, KD + k, 0:1]).then_inc(sem("h_full"), 1)
                    act.activation(hf[:, k % 2, 512:640], ps[:, b0 + 1, 0:P], ACT.Identity,
                                   bias=modc[:, k, 1:2], scale=modc[:, KD + k, 1:2]).then_inc(sem("h_full"), 1)
                    act.wait_ge(sem("h_full"), at("h_full", l, 2 * k + 2))
                    act.activation(actHk[:, k, :], hf[:, k % 2, :], ACT.Copy).then_inc(sem("h_hi"), 1)
                for i in range(3):
                    split_hi(i)
                for i in range(2):
                    act.wait_ge(sem(f"piece_out{i}"), at(f"piece_out{i}", l, 96))
                act.wait_ge(sem("tabs"), at("tabs", l, 6))
                act.wait_ge(sem("params_loaded"), at("params_loaded", l, 17 * 16))
                done = 3
                for gi in range(4 * NT):
                    nb, t = divmod(gi, NT)
                    bank = ps[:, gi % 8, :]
                    if t == 0:
                        while done < min(8, 2 * nb + 4 + 1):
                            split_hi(done)
                            done += 1
                    act.wait_ge(sem("proj"), at("proj", l, gi + 1))
                    free = sem("proj_read")
                    if nb == 0:
                        if gi:
                            act.wait_ge(sem("ssqk"), at("ssqk", l, gi))
                        else:
                            act.wait_ge(sem("h_lo"), at("h_lo", l, KD))
                        act.activation(pbuf[:, 0:512], bank, ACT.Square).then_inc(sem("sq"), 1)
                        act.activation(mrg[:, t, 0:512], bank, ACT.Copy).then_inc(free, 1)
                    elif nb == 1:
                        j = t if t < CTX else CTXK
                        act.wait_ge(sem("ssqk"), at("ssqk", l, gi))
                        act.activation(pbuf[:, 0:P], bank[:, 0:P], ACT.Square).then_inc(sem("sq"), 1)
                        act.activation(kv[:, j, :], bank[:, 0:256], ACT.Copy).then_inc(sem("kv_raw"), 1)
                        act.activation(mrg[:, t, 512:768], bank[:, 256:512], ACT.Copy).then_inc(free, 1)
                    elif nb == 2:
                        act.activation(sv[:, t, :], bank[:, 0:256], ACT.Copy).then_inc(sem("sv_raw"), 1)
                        act.activation(mrg[:, t, 768:1024], bank[:, 256:512], ACT.Copy).then_inc(free, 1)
                    else:
                        act.activation(z[:, t, :], bank[:, 0:256], ACT.Copy).then_inc(free, 1)
                act.wait_ge(sem("z_done"), at("z_done", l, NT))
                act.wait_ge(sem("zpn_zero"), at("zpn_zero", l, 2))
                sh = sem("shifted")
                act.dma_start(zp[1:P, :, :], z[0:P - 1, :, :]).then_inc(sh, 16)
                act.dma_start(zp[0:1, 1:NLT, :], z[P - 1:P, 0:NLT - 1, :]).then_inc(sh, 16)
                act.dma_start(zn[0:P - 1, :, :], z[1:P, :, :]).then_inc(sh, 16)
                act.dma_start(zn[P - 1:P, 0:NLT - 1, :], z[0:1, 1:NLT, :]).then_inc(sh, 16)
                act.wait_ge(sem("k_final"), at("k_final", l, NT))
                act.dma_start(O["new_k"][0, l].rearrange("s h d -> s (h d)"), kv[:, CTXK, 0:P]).then_inc(sem("out_done"), 16)
                act.dma_start(O["new_v"][0, l].rearrange("s h d -> s (h d)"), kv[:, CTXK, P:]).then_inc(sem("out_done"), 16)
                act.wait_ge(sem("sgT_psum"), at("sgT_psum", l, 1))
                act.activation(sgT[:, :, :].rearrange("p g q -> p (g q)"), ps[:, 7, :], ACT.Copy).then_inc(sem("sgT_ready"), 1)
                for v in range(NKV):
                    act.activation(vv[v][:, :, 0:HD], kv[:, :, P + HD * v:P + HD * (v + 1)], ACT.Copy).then_inc(sem("v_hi"), 1)
                for j in range(NKEY):
                    if j >= 2:
                        act.wait_ge(sem("kT_psum"), at("kT_psum", l, j - 1))
                    kf = kv[:, j, 0:P].rearrange("p (v d) -> p v d", v=NKV)
                    act.activation(kdup[:, j % 2, :, 0:2, :], kf.unsqueeze(2).to_broadcast([P, NKV, 2, HD]), ACT.Copy
                                   ).then_inc(sem("k_hi"), 1)
                    if j >= 1:
                        act.wait_ge(sem("kT_psum"), at("kT_psum", l, j))
                        act.activation(kk[:, :, (j - 1) * P:j * P], ps[:, (j - 1) % 2, :].rearrange("p (c n) -> p c n", c=4),
                                       ACT.Copy).then_inc(sem("kk"), 1)
                act.wait_ge(sem("kT_psum"), at("kT_psum", l, NKEY))
                act.activation(kk[:, :, (NKEY - 1) * P:], ps[:, (NKEY - 1) % 2, :].rearrange("p (c n) -> p c n", c=4),
                               ACT.Copy).then_inc(sem("kk"), 1)
                for i in range(8, 11):
                    split_hi(i)

                def q_hi(t):
                    act.wait_ge(sem("q_final"), at("q_final", l, t + 1))
                    if t:
                        act.wait_ge(sem("qT_psum"), at("qT_psum", l, 2 * t))
                    act.activation(qhl[:, :, 0, :], mrg[:, t, 0:512].rearrange("p (h d) -> p h d", h=NH), ACT.Copy
                                   ).then_inc(sem("q_hi"), 1)

                def q_out(t, r):
                    act.wait_ge(sem("qT_psum"), at("qT_psum", l, 2 * t + r + 1))
                    act.activation(qT[:, t % 2, 4 * r:4 * r + 4, :].rearrange("p h n -> p (h n)"), ps[:, 7, :], ACT.Copy
                                   ).then_inc(sem("qT"), 1)

                def o_low(g):
                    t, r = divmod(g, 2)
                    act.wait_ge(sem("pv"), at("pv", l, 4 * g + 4))
                    act.activation(mrg[:, t, 256 * r:256 * r + 256].rearrange("p (h d) -> p h d", h=4),
                                   ps[:, 6, :].rearrange("p (h s d) -> p h s d", h=4, s=2)[:, :, 1, :], ACT.Copy
                                   ).then_inc(sem("o_low"), 1)

                act.wait_ge(sem("kT_psum"), at("kT_psum", l, NKEY))
                q_hi(0)
                q_out(0, 0)
                q_out(0, 1)
                for u in range(NT * NH + 1):
                    if u < NT * NH:
                        t, h = divmod(u, NH)
                        keys = 5 * P if t < CTX else P
                        act.wait_ge(sem("nmax"), at("nmax", l, u + 1))
                        if u >= 2:
                            act.wait_ge(sem("pT_psum"), at("pT_psum", l, u - 1))
                        act.activation(prob[:, u % 2, 0:keys], ps[:, 2 * (u % 2):2 * (u % 2) + 2, :].rearrange(
                            "p b n -> p (b n)")[:, 0:keys], ACT.Exp, bias=nmax[:, u % 2:u % 2 + 1],
                            accum_out=rsum[:, u % 16:u % 16 + 1]).then_inc(sem("prob"), 1)
                        if h == 1 and t + 1 < NT:
                            q_hi(t + 1)
                        if h == 4 and t + 1 < NT:
                            q_out(t + 1, 0)
                        if h == 7 and t + 1 < NT:
                            q_out(t + 1, 1)
                    if u >= 1:
                        v = u - 1
                        keys = 5 * P if v < NLT * NH else P
                        act.wait_ge(sem("pT_psum"), at("pT_psum", l, v + 1))
                        if v >= 2:
                            act.wait_ge(sem("pv"), at("pv", l, v - 1))
                        act.activation(pTH[:, v % 2, 0:keys], ps[:, 4:6, :].rearrange("p b n -> p (b n)")[:, 0:keys],
                                       ACT.Copy).then_inc(sem("pT_hi"), 1)
                    if u >= 2 and (u - 2) % 4 == 3:
                        o_low((u - 2) // 4)
                o_low(2 * NT - 1)
                act.wait_ge(sem("attn_done"), at("attn_done", l, 2 * NT))
                act.wait_ge(sem("conv_done"), at("conv_done", l, 1))
                act.wait_ge(sem("sgu_done"), at("sgu_done", l, 4))
                for t in range(NT):
                    for j, (a, b) in enumerate(((0, 512), (512, 768), (768, 1024))):
                        if 3 * t + j:
                            act.wait_ge(sem("ss3"), at("ss3", l, 3 * t + j))
                        act.activation(pbuf[:, 0:b - a], mrg[:, t, a:b], ACT.Square,
                                       accum_out=stat[:, 32 + 5 * j + t:33 + 5 * j + t]).then_inc(sem("ss3"), 1)
                for k in range(KD):
                    act.wait_ge(sem("mT_psum"), at("mT_psum", l, k + 1))
                    b0 = 2 * (k % 2)
                    on = cols[:, KD + k:KD + k + 1]
                    act.activation(actHk[:, k, 0:512], ps[:, b0, :], ACT.Identity, scale=on).then_inc(sem("mT_hi"), 1)
                    act.activation(actHk[:, k, 512:640], ps[:, b0 + 1, 0:P], ACT.Identity, scale=on).then_inc(sem("mT_hi"), 1)
                split_hi(11)
                act.wait_ge(sem("out_done"), 32 * (l + 1))
                for t in range(NT):
                    act.wait_ge(sem("x_attn"), at("x_attn", l, NT + t + 1))
                    if t:
                        act.wait_ge(sem("ss2"), at("ss2", l, t))
                    act.activation(yb, x[:, t, :], ACT.Square, accum_out=stat[:, t:t + 1]).then_inc(sem("ss2"), 1)
                for t in range(NT):
                    act.wait_ge(sem("h2T_psum"), at("h2T_psum", l, t + 1))
                    act.dma_start(h2s[l][t * P:(t + 1) * P, :], h2b[:, t % 2, :]).then_inc(sem(f"h2_stored{t % 2}"), 16)
                    if t:
                        act.wait_ge(sem("logits"), at("logits", l, t))
                    b0 = 2 * (t % 2)
                    act.activation(h2T.rearrange("p k n -> p (k n)"), ps[:, b0:b0 + 2, :].rearrange("p b n -> p (b n)"),
                                   ACT.Copy).then_inc(sem("h2T"), 1)
                for i in range(2):
                    act.wait_ge(sem("rt_exp_in"), at("rt_exp_in", l, i + 1))
                    e_ = (ex, d_)[i]
                    act.activation(e_, e_, ACT.Exp).then_inc(sem("rt_exp"), 1)

                def m_split(i, b):
                    act.wait_ge(S(f"m_raw{i}", l), (b + 1) * (32 if i < 2 else 16))
                    act.activation(wH[:, i, :], raw[:, i, :], ACT.Copy).then_inc(S("m_hi", l), 1)

                def x_hi(b):
                    act.wait_ge(S("m_tx", l), b + 1)
                    act.activation(actH[:, 0:1024], ps[:, 1:3, :].rearrange("p b n -> p (b n)"), ACT.Copy
                                   ).then_inc(S("m_xh", l), 1)

                def block_body(b, last):
                    act.wait_ge(S("m_w13", l), b * 2 + 2)
                    act.activation(hid[:, 0:F], ps[:, 0, 0:F], ACT.Silu).then_inc(S("m_sg", l), 1)
                    if not last:
                        x_hi(b + 1)
                    act.wait_ge(S("m_th", l), b + 1)
                    act.activation(hTH.rearrange("p k n -> p (k n)"), ps[:, 3, 0:F], ACT.Copy).then_inc(S("m_hh", l), 1)
                    if not last:
                        m_split(0, b + 1)
                        m_split(1, b + 1)
                    act.wait_ge(S("m_w2", l), b + 1)
                    act.wait_ge(S("m_ys", l), b * 16 + 16)
                    act.activation(yb[:, 0:N], ps[:, 4, :], ACT.Copy).then_inc(S("m_ya", l), 1)
                    if not last:
                        m_split(2, b + 1)

                act.wait_ge(sem("ctl_ready"), at("ctl_ready", l, 1))
                last = act.value_load(ctl[0:1, 0:1], min_val=1, max_val=MAXB - 1)
                w_read(act, l, 11)
                act.sem_inc(S("m_ya", l), 1)
                x_hi(0)
                for i in range(3):
                    m_split(i, 0)
                with act.Fori(0, last) as b:
                    block_body(b, False)
                block_body(last, True)

            for t in range(NT):
                act.wait_ge(sem("x_moe"), at("x_moe", DEPTH, 0))
                if t:
                    act.wait_ge(sem("ssf"), t)
                act.activation(yb, x[:, t, :], ACT.Square, accum_out=stat[:, t:t + 1]).then_inc(sem("ssf"), 1)
            for t in range(NT):
                act.wait_ge(sem("y_final"), t + 1)
                dst = O["y_sample"][0, t * P:(t + 1) * P, :] if t < CTX else O["y_prompt"][0]
                act.dma_start(dst, x[:, t, :]).then_inc(sem("out_done"), 16)
            act.wait_ge(sem("out_done"), 16 * (NT + 2 * DEPTH))

        @block.vector
        def _(dve):
            steps = [0]

            def link(ins):
                steps[0] += 1
                ins.then_inc(sem("dve_step"), 1)
                dve.wait_ge(sem("dve_step"), steps[0])

            def bc(ap, n):
                return ap.unsqueeze(len(ap.shape)).to_broadcast([*ap.shape, n])

            def mid(ap, n):
                return ap.unsqueeze(1).to_broadcast([P, n, *ap.shape[1:]])

            dve.wait_ge(sem("consts_loaded"), 48)
            dve.tensor_copy(upper[:, :], rt[:, 0:P]).then_inc(sem("upper_ready"), 1)
            dve.memset(ones[:, :], 1.0).then_inc(sem("upper_ready"), 1)
            dve.wait_ge(sem("upper_ready"), 2)

            for l in range(DEPTH):
                def split_lo(i):
                    dve.wait_ge(sem("w_hi"), at("w_hi", l, i + 1))
                    dve.tensor_tensor(wL[:, i % HLS, :], raw[:, units[("w", i)] % RAWS, :], f32(wH[:, i % HLS, :]),
                                      ALU.subtract).then_inc(sem("w_lo"), 1)

                dve.wait_ge(sem("params_loaded"), at("params_loaded", l, 17 * 16))
                link(dve.tensor_scalar(gains[:, 0, :], gains[:, 0, :], float(HD) ** -0.5, None, ALU.mult))
                for qk in range(2):
                    dve.tensor_tensor(tabs[:, :, qk, 0, :], rtab[:, :, 0, :], mid(gains[:, qk, :], NT), ALU.mult
                                      ).then_inc(sem("tabs"), 1)
                    for half in range(2):
                        v5 = lambda ap: ap.rearrange("p t (x h f) -> p t x h f", x=2, h=2)[:, :, :, half, :]
                        gsw = gains[:, qk, :].rearrange("p (x h f) -> p x h f", x=2, h=2)[:, :, 1 - half, :]
                        dve.tensor_tensor(v5(tabs[:, :, qk, 1, :]), v5(rtab[:, :, 1, :]), mid(gsw, NT), ALU.mult
                                          ).then_inc(sem("tabs"), 1)
                for g in range(12):
                    if g == 4:
                        dve.wait_ge(sem("modc_psum"), at("modc_psum", l, 1))
                        link(dve.tensor_copy(modc[:, :, :].rearrange("p k c -> p (k c)"), ps[:, 5, 0:32]))
                        dve.scalar_tensor_tensor(out=modc[:, KD:, :], in0=modc[:, KD:, :], scalar=1.0,
                                                 in1=bc(cols[:, 0:KD], 2), op0=ALU.add, op1=ALU.mult
                                                 ).then_inc(sem("a1_ready"), 1)
                        dve.wait_ge(sem("rstd1"), at("rstd1", l, 1))
                        for t in range(NT):
                            dve.tensor_scalar(xr[:, t, :], x[:, t, :], stat[:, 8 + t:9 + t], None, ALU.mult
                                              ).then_inc(sem("xr_ready"), 1)
                    dve.wait_ge(sem("ada_read"), at("ada_read", l, 2 * g + 2))
                    dve.wait_ge(sem(f"bias_in{g % 2}"), at(f"bias_in{g % 2}", l, 16 * (g // 2 + 1)))
                    if g >= 2:
                        dve.wait_ge(sem(f"piece_out{g % 2}"), at(f"piece_out{g % 2}", l, 16 * (g // 2)))
                        if g < 5:
                            dve.wait_ge(sem("modc_part"), at("modc_part", l, g - 1))
                        elif g == 5:
                            dve.wait_ge(sem("modc_psum"), at("modc_psum", l, 1))
                    add = dve.tensor_tensor(piece[:, g % 2, :], ps[0:2, 6 + g % 2, :], bpiece[:, g % 2, :], ALU.add)
                    if g in (8, 9):
                        link(add)
                        dve.wait_ge(sem("norm2_in"), at("norm2_in", l, 32))
                        add = dve.scalar_tensor_tensor(out=piece[:, g % 2, :], in0=piece[:, g % 2, :], scalar=1.0,
                                                       in1=npiece[:, g - 8, :], op0=ALU.add, op1=ALU.mult)
                    add.then_inc(sem("piece_done"), 1)
                for k in range(KD):
                    dve.wait_ge(sem("h_hi"), at("h_hi", l, k + 1))
                    dve.tensor_tensor(actLk[:, k, :], hf[:, k % 2, :], f32(actHk[:, k, :]), ALU.subtract
                                      ).then_inc(sem("h_lo"), 1)
                for i in range(3):
                    split_lo(i)
                dve.wait_ge(sem("tabs"), at("tabs", l, 6))
                done = 3
                for gi in range(4 * NT):
                    nb, t = divmod(gi, NT)
                    if t == 0:
                        while done < min(8, 2 * nb + 4 + 1):
                            split_lo(done)
                            done += 1
                    if nb < 2:
                        H = NH if nb == 0 else NKV
                        final = "q_final" if nb == 0 else "k_final"
                        j = t if t < CTX else CTXK
                        W = H * HD
                        src = mrg[:, t, 0:512] if nb == 0 else kv[:, j, 0:P]
                        heads = lambda ap: ap.rearrange("p (h d) -> p h d", d=HD)
                        half = lambda ap, i: ap.rearrange("p (x h f) -> p x h f", h=2, f=16)[:, :, i, :]
                        t1, t2 = pbuf[:, 512:512 + W], pbuf[:, 1024:1024 + W]
                        dve.wait_ge(sem("sq"), at("sq", l, gi + 1))
                        dve.reduce_sum(stat[:, 16:16 + H], heads(pbuf[:, 0:W]), X).then_inc(sem("ssqk"), 1)
                        dve.wait_ge(sem("rqk"), at("rqk", l, gi + 1))
                        dve.wait_ge(sem("proj_read"), at("proj_read", l, gi + 1))
                        if nb == 1:
                            dve.wait_ge(sem("kv_raw"), at("kv_raw", l, t + 1))
                        link(dve.tensor_tensor(heads(src), heads(src), bc(stat[:, 24:24 + H], HD), ALU.mult))
                        link(dve.tensor_tensor(heads(t1), heads(src), mid(tabs[:, t, nb, 0, :], H), ALU.mult))
                        for i in range(2):
                            sn = tabs[:, t, nb, 1, :].rearrange("p (x h f) -> p x h f", x=2, h=2)[:, :, i, :]
                            o4 = t2.rearrange("p (n x h f) -> p n x h f", x=2, h=2, f=16)[:, :, :, i, :]
                            i4 = src.rearrange("p (n x h f) -> p n x h f", x=2, h=2, f=16)[:, :, :, 1 - i, :]
                            link(dve.tensor_tensor(o4, i4, mid(sn, H), ALU.mult))
                        dve.tensor_tensor(src, t1, t2, ALU.add).then_inc(sem(final), 1)
                        dve.wait_ge(sem(final), at(final, l, t + 1))
                    elif nb == 3:
                        dve.wait_ge(sem("proj_read"), at("proj_read", l, gi + 1))
                        dve.tensor_tensor(z[:, t, :], z[:, t, :], ps[:, gi % 8, 256:512], ALU.mult
                                          ).then_inc(sem("z_done"), 1)
                for v in range(NKV):
                    dve.wait_ge(sem("v_hi"), at("v_hi", l, v + 1))
                    dve.tensor_tensor(vv[v][:, :, HD:], kv[:, :, P + HD * v:P + HD * (v + 1)], f32(vv[v][:, :, 0:HD]),
                                      ALU.subtract).then_inc(sem("v_lo"), 1)
                for j in range(NKEY):
                    dve.wait_ge(sem("k_hi"), at("k_hi", l, j + 1))
                    kf = kv[:, j, 0:P].rearrange("p (v d) -> p v d", v=NKV)
                    dve.tensor_tensor(kdup[:, j % 2, :, 2:4, :], kf.unsqueeze(2).to_broadcast([P, NKV, 2, HD]),
                                      f32(kdup[:, j % 2, :, 0:2, :]), ALU.subtract).then_inc(sem("k_lo"), 1)
                for g in range(4):
                    dve.wait_ge(sem("sgu_psum"), at("sgu_psum", l, g + 1))
                    u_ = mrg[:, :, 512 + 64 * g:576 + 64 * g]
                    dve.scalar_tensor_tensor(out=u_, in0=ps[:, 2 + g, 0:320].rearrange("p (t c) -> p t c", t=NT),
                                             scalar=sgb[:, g:g + 1], in1=u_, op0=ALU.add, op1=ALU.mult
                                             ).then_inc(sem("sgu_done"), 1)
                dve.wait_ge(sem("shifted"), at("shifted", l, 64))
                link(dve.tensor_tensor(zp[:, :, :], zp[:, :, :], mid(cw[:, 0, :], NT), ALU.mult))
                link(dve.tensor_tensor(z[:, :, :], z[:, :, :], mid(cw[:, 1, :], NT), ALU.mult))
                link(dve.tensor_tensor(z[:, :, :], z[:, :, :], zp[:, :, :], ALU.add))
                dve.wait_ge(sem("tap2"), at("tap2", l, 1))
                link(dve.tensor_tensor(z[:, :, :], z[:, :, :], zn[:, :, :], ALU.add))
                dve.tensor_tensor(mrg[:, :, 768:], mrg[:, :, 768:], z[:, :, :], ALU.mult).then_inc(sem("conv_done"), 1)
                for i in range(8, 11):
                    split_lo(i)

                def q_lo(t):
                    dve.wait_ge(sem("q_hi"), at("q_hi", l, t + 1))
                    dve.tensor_tensor(qhl[:, :, 1, :], mrg[:, t, 0:512].rearrange("p (h d) -> p h d", h=NH),
                                      f32(qhl[:, :, 0, :]), ALU.subtract).then_inc(sem("q_lo"), 1)

                def o_high(g):
                    t, r = divmod(g, 2)
                    dst = mrg[:, t, 256 * r:256 * r + 256].rearrange("p (h d) -> p h d", h=4)
                    dve.wait_ge(sem("o_low"), at("o_low", l, g + 1))
                    c = (8 * t + 4 * r) % 16
                    link(dve.reciprocal(rinv[:, 4 * r:4 * r + 4], rsum[:, c:c + 4]))
                    dve.tensor_tensor(dst, ps[:, 6, :].rearrange("p (h s d) -> p h s d", h=4, s=2)[:, :, 0, :], dst,
                                      ALU.add).then_inc(sem("o_read"), 1)
                    dve.wait_ge(sem("o_read"), at("o_read", l, g + 1))
                    dve.tensor_tensor(dst, dst, bc(rinv[:, 4 * r:4 * r + 4], HD), ALU.mult).then_inc(sem("attn_done"), 1)

                q_lo(0)
                for u in range(NT * NH + 1):
                    if u < NT * NH:
                        t, h = divmod(u, NH)
                        keys = 5 * P if t < CTX else P
                        dve.wait_ge(sem("scores"), at("scores", l, u + 1))
                        if u >= 2:
                            dve.wait_ge(sem("prob"), at("prob", l, u - 1))
                        dve.tensor_reduce(nmax[:, u % 2:u % 2 + 1], ps[:, 2 * (u % 2):2 * (u % 2) + 2, :].rearrange(
                            "p b n -> p (b n)")[:, 0:keys], X, ALU.max, negate=True).then_inc(sem("nmax"), 1)
                        if h == 2 and t + 1 < NT:
                            q_lo(t + 1)
                    if u >= 1:
                        v = u - 1
                        keys = 5 * P if v < NLT * NH else P
                        dve.wait_ge(sem("pT_hi"), at("pT_hi", l, v + 1))
                        dve.tensor_tensor(pTL[:, v % 2, 0:keys], ps[:, 4:6, :].rearrange("p b n -> p (b n)")[:, 0:keys],
                                          f32(pTH[:, v % 2, 0:keys]), ALU.subtract).then_inc(sem("pT_lo"), 1)
                    if u >= 2 and (u - 2) % 4 == 3:
                        o_high((u - 2) // 4)
                o_high(2 * NT - 1)
                dve.wait_ge(sem("rstd3"), at("rstd3", l, 1))
                dve.wait_ge(sem("attn_done"), at("attn_done", l, 2 * NT))
                for t in range(NT):
                    for j, (a, b) in enumerate(((0, 512), (512, 768), (768, 1024))):
                        c = 48 + 5 * j + t
                        dve.tensor_scalar(mrg[:, t, a:b], mrg[:, t, a:b], stat[:, c:c + 1], None, ALU.mult
                                          ).then_inc(sem("mrg_ready"), 1)
                for k in range(KD):
                    dve.wait_ge(sem("mT_hi"), at("mT_hi", l, 2 * k + 2))
                    b0 = 2 * (k % 2)
                    on = cols[:, KD + k:KD + k + 1]
                    dve.scalar_tensor_tensor(out=actLk[:, k, 0:512], in0=ps[:, b0, :], scalar=on, in1=f32(actHk[:, k, 0:512]),
                                             op0=ALU.mult, op1=ALU.subtract).then_inc(sem("mT_lo"), 1)
                    dve.scalar_tensor_tensor(out=actLk[:, k, 512:640], in0=ps[:, b0 + 1, 0:P], scalar=on,
                                             in1=f32(actHk[:, k, 512:640]), op0=ALU.mult, op1=ALU.subtract
                                             ).then_inc(sem("mT_lo"), 1)
                split_lo(11)
                dve.wait_ge(sem("gate1_row"), at("gate1_row", l, 32))
                dve.wait_ge(sem("mT_psum"), at("mT_psum", l, KD))
                for i in range(2 * NT):
                    nb, t = divmod(i, NT)
                    dve.wait_ge(sem("oproj_psum"), at("oproj_psum", l, i + 1))
                    if i >= 4:
                        dve.wait_ge(sem("x_attn"), at("x_attn", l, i - 3))
                    dve.tensor_tensor(otmp[:, i % 4, :], ps[:, i % 8, :], grow[:, int(t == CTX), nb * N:(nb + 1) * N],
                                      ALU.mult).then_inc(sem("oproj"), 1)
                dve.wait_ge(sem("scale2_row"), at("scale2_row", l, 32))
                dve.wait_ge(sem("shift2_row"), at("shift2_row", l, 32))
                for t in range(NT):
                    c = int(t == CTX)
                    dve.wait_ge(sem("rstd2"), at("rstd2", l, t + 1))
                    dve.wait_ge(sem("x_attn"), at("x_attn", l, 2 * NT))
                    if t >= 2:
                        dve.wait_ge(sem(f"h2_stored{t % 2}"), at(f"h2_stored{t % 2}", l, 16 * (t // 2)))
                        dve.wait_ge(sem("h2T_psum"), at("h2T_psum", l, t - 1))
                    hb = h2b[:, t % 2, :]
                    link(dve.scalar_tensor_tensor(out=hb, in0=x[:, t, :], scalar=stat[:, 8 + t:9 + t], in1=arow[:, c, :],
                                                  op0=ALU.mult, op1=ALU.mult))
                    dve.tensor_tensor(hb, hb, srow[:, c, :], ALU.add).then_inc(sem("h2"), 1)
                dve.wait_ge(sem("ss2"), at("ss2", l, NT))

                dve.wait_ge(sem("logits"), at("logits", l, NT))
                pri, thr, bidx = pcon[:, 0:4], pcon[:, 4:9], pcon[:, 9:9 + LB]
                tidx, toff = pcon[:, 40:41], pcon[:, 41:46]
                link(dve.tensor_tensor(lg, ps[:, 4, 0:100].rearrange("p (t n) -> p t n", t=NT), mid(rb[:, :], NT), ALU.add))
                gl, el = lg[:, :, 0:NG], lg[:, :, NG:]

                def first_max(v, m, out):
                    link(dve.tensor_reduce(m, v, X, ALU.max))
                    link(dve.tensor_tensor(eq, v, bc(m, 4), ALU.is_equal))
                    link(dve.tensor_tensor(eq, eq, mid(pri, NT), ALU.mult))
                    link(dve.tensor_reduce(sm, eq, X, ALU.max))
                    link(dve.tensor_tensor(out, eq, bc(sm, 4), ALU.is_equal))

                first_max(gl, gm, og)
                dve.tensor_tensor(ex, gl, bc(gm, 4), ALU.subtract).then_inc(sem("rt_exp_in"), 1)
                link(dve.tensor_tensor(pr, el.rearrange("p t (g e) -> p t g e", g=4), bc(og, 4), ALU.mult))
                link(dve.reduce_sum(es, pr.rearrange("p t g e -> p t e g"), X))
                first_max(es, em1, o1)
                link(dve.scalar_tensor_tensor(out=e2, in0=o1, scalar=-1e30, in1=es, op0=ALU.mult, op1=ALU.add))
                first_max(e2, em2, o2)
                dve.wait_ge(sem("rt_exp"), at("rt_exp", l, 1))
                link(dve.reduce_sum(pg, ex, X))
                link(dve.reciprocal(pg, pg))
                dve.tensor_tensor(d_, em2, em1, ALU.subtract).then_inc(sem("rt_exp_in"), 1)
                for c, o in enumerate((o1, o2)):
                    link(dve.tensor_tensor(M[:, c].rearrange("p t (g e) -> p t g e", g=4), bc(og, 4),
                                           o.unsqueeze(2).to_broadcast([P, NT, 4, 4]), ALU.mult))
                dve.tensor_tensor(Mb, M[:, 0], M[:, 1], ALU.add).then_inc(sem("choice"), 1)
                dve.wait_ge(sem("rt_exp"), at("rt_exp", l, 2))
                link(dve.tensor_scalar(em1, d_, 1.0, None, ALU.add))
                link(dve.reciprocal(em1, em1))
                link(dve.tensor_tensor(gate[:, 0, :], em1, pg, ALU.mult))
                link(dve.tensor_tensor(gate[:, 1, :], gate[:, 0, :], d_, ALU.mult))
                dve.wait_ge(sem("counts_psum"), at("counts_psum", l, 1))
                link(dve.tensor_copy(pos, ps[:, 5, 0:NT * 16]))
                link(dve.tensor_copy(cnt, ps[:, 6, 0:16]))
                link(dve.tensor_tensor(cmp5, bc(cnt, 5), mid(thr, 16), ALU.is_gt))
                link(dve.reduce_sum(nb_, cmp5, X))
                link(dve.tensor_tensor_scan(incl, pcon[:, 46:62], nb_, 0.0, ALU.mult, ALU.add))
                link(dve.tensor_tensor(base, incl, nb_, ALU.subtract))
                Mf = M.rearrange("p c t e -> p c (t e)")
                link(dve.tensor_tensor(pr2.rearrange("p (c n) -> p c n", c=2), Mf, mid(pos, 2), ALU.mult))
                link(dve.reduce_sum(q, pr2.rearrange("p (c e) -> p c e", e=16), X))
                M10 = M.rearrange("p c t e -> p (c t) e")
                link(dve.tensor_tensor(pr2.rearrange("p (c e) -> p c e", e=16), M10, mid(base, 10), ALU.mult))
                link(dve.reduce_sum(eb, pr2.rearrange("p (c e) -> p c e", e=16), X))
                link(dve.tensor_tensor(pr2[:, 0:40].rearrange("p (c e) -> p c e", e=4), bc(q, 4), mid(thr[:, 1:5], 10), ALU.is_ge))
                link(dve.reduce_sum(qd, pr2[:, 0:40].rearrange("p (c e) -> p c e", e=4), X))
                link(dve.tensor_tensor(eb, eb, qd, ALU.add))
                link(dve.scalar_tensor_tensor(out=q, in0=qd, scalar=-128.0, in1=q, op0=ALU.mult, op1=ALU.add))
                link(dve.scalar_tensor_tensor(out=qd, in0=eb, scalar=128.0, in1=q, op0=ALU.mult, op1=ALU.add))
                link(dve.tensor_copy(slot[:, :], qd))
                link(dve.tensor_tensor(one_r, bc(q, P), mid(iota[:, :], 10), ALU.is_equal))
                link(dve.tensor_tensor(oneb, bc(eb, LB), mid(bidx, 10), ALU.is_equal))
                link(dve.tensor_scalar(tl[:, :, 0, :], oneb, tidx, None, ALU.mult))
                for c in range(2):
                    link(dve.tensor_tensor(tl[:, c * NT:(c + 1) * NT, 1, :], oneb[:, c * NT:(c + 1) * NT, :], bc(toff, LB), ALU.mult))
                dve.sem_inc(sem("lists"), 1)
                for i in range(3):
                    n = min(10, LB - 10 * i)
                    cbv = pr2[:, 0:16 * n].rearrange("p (b e) -> p b e", e=16)
                    link(dve.tensor_tensor(cbv, mid(incl, n), bc(bidx[:, 10 * i:10 * i + n], 16), ALU.is_le))
                    link(dve.reduce_sum(eb26[:, 1 + 10 * i:1 + 10 * i + n], cbv, X))
                link(dve.tensor_scalar(eb26[:, 1:1 + LB], eb26[:, 1:1 + LB], float(NE - 1), None, ALU.min))
                link(dve.tensor_scalar(eb26[:, 0:1], incl[:, 15:16], -1.0, None, ALU.add))
                link(dve.tensor_copy(ctl[0:1, 0:1 + LB], eb26[0:1, 0:1 + LB]))
                dve.wait_ge(sem("list_psum"), at("list_psum", l, 1))
                idf, empt = pr2[:, 0:2 * LB].rearrange("p (s b) -> p s b", s=2), pr2[:, 2 * LB:3 * LB]
                link(dve.tensor_copy(idf.rearrange("p s b -> p (s b)"), ps[:, 7, 0:2 * LB]))
                link(dve.tensor_scalar(empt, idf[:, 0, :], 0.0, float(NOROW), ALU.is_equal, ALU.mult))
                link(dve.scalar_tensor_tensor(out=idf[:, 0, :], in0=idf[:, 0, :], scalar=-1.0, in1=idf[:, 1, :],
                                              op0=ALU.add, op1=ALU.add))
                link(dve.tensor_tensor(idf[:, 0, :], idf[:, 0, :], empt, ALU.add))
                link(dve.tensor_scalar(idf[:, 0, :], idf[:, 0, :], 0.0, None, ALU.max))
                link(dve.tensor_copy(idxs[:, :], idf[:, 0, :]))
                link(dve.memset(xg, 0.0))
                dve.sem_inc(sem("xg_zero"), 1)
                dve.sem_inc(sem("ctl_ready"), 1)

                def m_split(i, b):
                    dve.wait_ge(S("m_hi", l), 3 * b + i + 1)
                    dve.tensor_tensor(wL[:, i, :], raw[:, i, :], f32(wH[:, i, :]), ALU.subtract).then_inc(S("m_lo", l), 1)

                def x_lo(b):
                    dve.wait_ge(S("m_xh", l), b + 1)
                    dve.tensor_tensor(actL[:, 0:1024], ps[:, 1:3, :].rearrange("p b n -> p (b n)"), f32(actH[:, 0:1024]),
                                      ALU.subtract).then_inc(S("m_xl", l), 1)

                def block_body(b, last):
                    dve.wait_ge(S("m_sg", l), b + 1)
                    dve.tensor_tensor(hid[:, F:2 * F], hid[:, 0:F], ps[:, 0, F:2 * F], ALU.mult).then_inc(S("m_hid", l), 1)
                    if not last:
                        x_lo(b + 1)
                    dve.wait_ge(S("m_hh", l), b + 1)
                    dve.tensor_tensor(hTL.rearrange("p k n -> p (k n)"), ps[:, 3, 0:F], f32(hTH.rearrange("p k n -> p (k n)")),
                                      ALU.subtract).then_inc(S("m_hl", l), 1)
                    if not last:
                        m_split(0, b + 1)
                        m_split(1, b + 1)
                    dve.wait_ge(S("m_w2", l), b + 1)
                    dve.wait_ge(S("m_ys", l), b * 16 + 16)
                    dve.tensor_copy(yb[:, N:], ps[:, 5, :]).then_inc(S("m_yd", l), 1)
                    if not last:
                        m_split(2, b + 1)

                last = dve.value_load(ctl[0:1, 0:1], min_val=1, max_val=MAXB - 1)
                dve.sem_inc(S("m_yd", l), 1)
                dve.sem_inc(S("m_ys", l), 16)
                x_lo(0)
                for i in range(3):
                    m_split(i, 0)
                with dve.Fori(0, last) as b:
                    block_body(b, False)
                block_body(last, True)
                dve.sem_inc(sem("moe_split_done"), 1)
                dve.wait_ge(sem("gate2_row"), at("gate2_row", l, 32))
                for t in range(NT):
                    c = int(t == CTX)
                    y1, y2 = h2b[:, 0, :], h2b[:, 1, :]
                    dve.wait_ge(sem("y_in0"), at("y_in0", l, 16 * (t + 1)))
                    link(dve.tensor_scalar(yb, y1, gate[:, 0, t:t + 1], None, ALU.mult))
                    dve.sem_inc(sem("y_read"), 1)
                    dve.wait_ge(sem("y_in1"), at("y_in1", l, 16 * (t + 1)))
                    link(dve.scalar_tensor_tensor(out=yb, in0=y2, scalar=gate[:, 1, t:t + 1], in1=yb, op0=ALU.mult, op1=ALU.add))
                    dve.sem_inc(sem("y_read"), 1)
                    link(dve.tensor_tensor(yb, yb, grow[:, c, :], ALU.mult))
                    dve.tensor_tensor(x[:, t, :], x[:, t, :], yb, ALU.add).then_inc(sem("x_moe"), 1)
                    dve.wait_ge(sem("x_moe"), at("x_moe", l, t + 1))

            dve.wait_ge(sem("final_row"), 16)
            for t in range(NT):
                dve.wait_ge(sem("rstdf"), t + 1)
                dve.scalar_tensor_tensor(out=x[:, t, :], in0=x[:, t, :], scalar=stat[:, 8 + t:9 + t], in1=frow,
                                         op0=ALU.mult, op1=ALU.mult).then_inc(sem("y_final"), 1)

        @block.tensor
        def _(pe):
            pe.wait_ge(sem("c_silu"), 1)
            pe.wait_ge(sem("ident_loaded"), 16)

            def three(out, aH, aL, slot_, cols_, first, last):
                pe.matmul(out, aH, wH[:, slot_, cols_], start=first, stop=False)
                pe.matmul(out, aH, wL[:, slot_, cols_], start=False, stop=False)
                return pe.matmul(out, aL, wH[:, slot_, cols_], start=False, stop=last)

            for l in range(DEPTH):
                for g in range(12):
                    if g >= 2:
                        pe.wait_ge(sem("piece_done"), at("piece_done", l, g - 1))
                    for half in range(2):
                        i = units[("ada", 2 * g + half)]
                        unit_loaded(pe, l, i)
                        w = raw[:, i % RAWS, :].rearrange("p (k n) -> p k n", k=4)
                        for k in range(4):
                            kt = 4 * half + k
                            m = pe.matmul(ps[0:2, 6 + g % 2, :], csil[:, kt, :], w[:, k, :], start=(kt == 0), stop=(kt == KD - 1))
                            if k == 3:
                                m.then_inc(sem("ada_read"), 1)
                    if g < 4:
                        pe.wait_ge(sem("piece_done"), at("piece_done", l, g + 1))
                        for j in range(4):
                            m = pe.transpose(ps[:, 5, 8 * g + 2 * j:8 * g + 2 * j + 2], piece[:, g % 2, j * P:(j + 1) * P],
                                             ident[0:2, 0:2])
                        m.then_inc(sem("modc_psum" if g == 3 else "modc_part"), 1)
                pe.wait_ge(sem("xr_ready"), at("xr_ready", l, NT))
                for k in range(KD):
                    if k >= 2:
                        pe.wait_ge(sem("h_full"), at("h_full", l, 2 * k - 2))
                    for t in range(NT):
                        m = pe.transpose(ps[:, 2 * (k % 2) + t // 4, P * (t % 4):P * (t % 4) + P], xr[:, t, k * P:(k + 1) * P], ident[:, :])
                    m.then_inc(sem("hT_psum"), 1)
                pe.wait_ge(sem("h_lo"), at("h_lo", l, KD))
                pe.wait_ge(sem("piece_done"), at("piece_done", l, 12))
                for i in range(8):
                    nb, half = divmod(i, 2)
                    pe.wait_ge(sem("w_lo"), at("w_lo", l, i + 1))
                    for k in range(4):
                        kt = 4 * half + k
                        for t in range(NT):
                            gi = nb * NT + t
                            if kt == 0 and gi >= 8:
                                pe.wait_ge(sem("proj_read"), at("proj_read", l, gi - 7))
                            m = three(ps[:, gi % 8, :], actHk[:, kt, t * P:(t + 1) * P], actLk[:, kt, t * P:(t + 1) * P],
                                      i % HLS, slice(k * N, (k + 1) * N), kt == 0, kt == KD - 1)
                            if kt == KD - 1:
                                m.then_inc(sem("proj"), 1)
                    if half == 0:
                        m.then_inc(sem("w_used"), 1)
                pe.wait_ge(sem("z_done"), at("z_done", l, NT))
                for g in range(4):
                    m = pe.transpose(ps[:, 7, g * P:(g + 1) * P], sgw[:, g, :], ident[:, :])
                m.then_inc(sem("sgT_psum"), 1)
                pe.wait_ge(sem("sgT_ready"), at("sgT_ready", l, 1))
                for g in range(4):
                    pe.matmul(ps[:, 2 + g, 0:320], sgT[:, g, :], sv[:, :, 64 * g:64 * g + 64], start=True, stop=True
                              ).then_inc(sem("sgu_psum"), 1)
                for j in range(NKEY):
                    pe.wait_ge(sem("k_lo"), at("k_lo", l, j + 1))
                    if j >= 2:
                        pe.wait_ge(sem("kk"), at("kk", l, j - 1))
                    for c in range(4):
                        kd = kdup[:, j % 2, :, :, :].rearrange("p v s d -> p (v s d)")
                        m = pe.transpose(ps[:, j % 2, c * P:(c + 1) * P], f32(kd[:, c * P:(c + 1) * P]), ident[:, :])
                    m.then_inc(sem("kT_psum"), 1)

                def q_round(t, r):
                    if r == 0:
                        pe.wait_ge(sem("q_lo"), at("q_lo", l, t + 1))
                    if t or r:
                        pe.wait_ge(sem("qT"), at("qT", l, 2 * t + r))
                    for h in range(4):
                        m = pe.transpose(ps[:, 7, h * P:(h + 1) * P],
                                         f32(qhl[:, 4 * r + h, :, :].rearrange("p s d -> p (s d)")), ident[:, :])
                    m.then_inc(sem("qT_psum"), 1)

                q_round(0, 0)
                q_round(0, 1)
                pe.wait_ge(sem("kk"), at("kk", l, NKEY))
                pe.wait_ge(sem("v_lo"), at("v_lo", l, NKV))
                pe.wait_ge(sem("sgu_done"), at("sgu_done", l, 4))
                for u in range(NT * NH + 2):
                    if u < NT * NH:
                        t, h = divmod(u, NH)
                        v, b0 = h // 4, 2 * (u % 2)
                        if h == 0:
                            pe.wait_ge(sem("qT"), at("qT", l, 2 * t + 2))
                        if u >= 2:
                            pe.wait_ge(sem("prob"), at("prob", l, u - 1))
                        spans = [(0, 0, 512), (1, 512, 640)] if t < CTX else [(0, 640, 768)]
                        for bk, a, b in spans:
                            pe.matmul(ps[:, b0 + bk, 0:b - a], qT[:, t % 2, h, :], kk[:, 2 * v, a:b], start=True, stop=False)
                            m = pe.matmul(ps[:, b0 + bk, 0:b - a], qT[:, t % 2, h, :], kk[:, 2 * v + 1, a:b], start=False, stop=True)
                        m.then_inc(sem("scores"), 1)
                        if h == 3 and t + 1 < NT:
                            q_round(t + 1, 0)
                        if h == 6 and t + 1 < NT:
                            q_round(t + 1, 1)
                    if 1 <= u <= NT * NH:
                        w = u - 1
                        nk = 5 if w < NLT * NH else 1
                        pe.wait_ge(sem("prob"), at("prob", l, w + 1))
                        if w:
                            pe.wait_ge(sem("pT_lo"), at("pT_lo", l, w))
                        for c in range(nk):
                            m = pe.transpose(ps[:, 4 + c // 4, (c % 4) * P:(c % 4) * P + P], prob[:, w % 2, c * P:(c + 1) * P], ident[:, :])
                        m.then_inc(sem("pT_psum"), 1)
                    if u >= 2:
                        w = u - 2
                        t, h = divmod(w, NH)
                        pe.wait_ge(sem("pT_lo"), at("pT_lo", l, w + 1))
                        if w % 4 == 0 and w:
                            pe.wait_ge(sem("o_read"), at("o_read", l, w // 4))
                        slots = range(5) if t < CTX else [CTXK]
                        o = (h % 4) * P
                        for c, j in enumerate(slots):
                            pe.matmul(ps[:, 6, o:o + P], pTH[:, w % 2, c * P:(c + 1) * P], vv[h // 4][:, j, :],
                                      start=(c == 0), stop=False, skip_group_check=True)
                            m = pe.matmul(ps[:, 6, o:o + HD], pTL[:, w % 2, c * P:(c + 1) * P], vv[h // 4][:, j, 0:HD],
                                          start=False, stop=(c == len(slots) - 1), skip_group_check=True)
                        m.then_inc(sem("pv"), 1)
                pe.wait_ge(sem("mrg_ready"), at("mrg_ready", l, 3 * NT))
                for k in range(KD):
                    if k >= 2:
                        pe.wait_ge(sem("mT_lo"), at("mT_lo", l, 2 * k - 2))
                    for t in range(NT):
                        m = pe.transpose(ps[:, 2 * (k % 2) + t // 4, P * (t % 4):P * (t % 4) + P], mrg[:, t, k * P:(k + 1) * P], ident[:, :])
                    m.then_inc(sem("mT_psum"), 1)
                pe.wait_ge(sem("mT_lo"), at("mT_lo", l, 2 * KD))
                for i in range(8, 12):
                    nb, half = divmod(i - 8, 2)
                    pe.wait_ge(sem("w_lo"), at("w_lo", l, i + 1))
                    for k in range(4):
                        kt = 4 * half + k
                        for t in range(NT):
                            gi = nb * NT + t
                            if kt == 0 and gi >= 8:
                                pe.wait_ge(sem("oproj"), at("oproj", l, gi - 7))
                            m = three(ps[:, gi % 8, :], actHk[:, kt, t * P:(t + 1) * P], actLk[:, kt, t * P:(t + 1) * P],
                                      i % HLS, slice(k * N, (k + 1) * N), kt == 0, kt == KD - 1)
                            if kt == KD - 1:
                                m.then_inc(sem("oproj_psum"), 1)
                    if half == 0:
                        m.then_inc(sem("w_used"), 1)
                pe.wait_ge(sem("oproj"), at("oproj", l, 2 * NT))
                for t in range(NT):
                    pe.wait_ge(sem("h2"), at("h2", l, t + 1))
                    if t >= 2:
                        pe.wait_ge(sem("h2T"), at("h2T", l, t - 1))
                    for k in range(KD):
                        m = pe.transpose(ps[:, 2 * (t % 2) + k // 4, (k % 4) * P:(k % 4) * P + P], h2b[:, t % 2, k * P:(k + 1) * P], ident[:, :])
                    m.then_inc(sem("h2T_psum"), 1)
                    pe.wait_ge(sem("h2T"), at("h2T", l, t + 1))
                    for k in range(KD):
                        m = pe.matmul(ps[:, 4, 20 * t:20 * t + 20], h2T[:, k, :], rw[:, k, :], start=(k == 0), stop=(k == KD - 1))
                    m.then_inc(sem("logits"), 1)
                pe.wait_ge(sem("choice"), at("choice", l, 1))
                pe.matmul(ps[:, 5, 0:NT * 16], upper[:, :], Mb, start=True, stop=False, skip_group_check=True)
                for t in range(NT - 1):
                    pe.matmul(ps[:, 5, (t + 1) * 16:NT * 16], ones[:, :], Mb[:, t, :].unsqueeze(1).to_broadcast([P, NT - 1 - t, 16]),
                              start=False, stop=(t == NT - 2), skip_group_check=True)
                for t in range(NT):
                    m = pe.matmul(ps[:, 6, 0:16], ones[:, :], Mb[:, t, :], start=(t == 0), stop=(t == NT - 1))
                m.then_inc(sem("counts_psum"), 1)
                pe.wait_ge(sem("lists"), at("lists", l, 1))
                for c in range(10):
                    m = pe.matmul(ps[:, 7, 0:2 * LB], one_r[:, c, :], tl[:, c, :, :].rearrange("p s b -> p (s b)"), start=(c == 0), stop=(c == 9))
                m.then_inc(sem("list_psum"), 1)

                def x_chunks(b):
                    pe.wait_ge(S("m_g", l), (b + 1) * 16)
                    for k in range(KD):
                        m = pe.transpose(ps[:, 1 + k // 4, (k % 4) * P:(k % 4) * P + P], xg[:, k * P:(k + 1) * P], ident[:, :])
                    m.then_inc(S("m_tx", l), 1)

                def block_body(b, last):
                    pe.wait_ge(S("m_xl", l), b + 1)
                    for half in range(2):
                        pe.wait_ge(S("m_lo", l), b * 3 + half + 1)
                        for k in range(4):
                            kt = 4 * half + k
                            m = three(ps[:, 0, :], xTH[:, kt, :], xTL[:, kt, :], half, slice(k * N, (k + 1) * N), kt == 0, kt == KD - 1)
                        m.then_inc(S("m_w13", l), 1)
                    if not last:
                        x_chunks(b + 1)
                    pe.wait_ge(S("m_hid", l), b + 1)
                    for k in range(2):
                        m = pe.transpose(ps[:, 3, k * P:(k + 1) * P], hid[:, F + k * P:F + (k + 1) * P], ident[:, :])
                    m.then_inc(S("m_th", l), 1)
                    pe.wait_ge(S("m_ya", l), b + 1)
                    pe.wait_ge(S("m_yd", l), b + 1)
                    pe.wait_ge(S("m_lo", l), b * 3 + 3)
                    pe.wait_ge(S("m_hl", l), b + 1)
                    for nb in range(2):
                        for k in range(2):
                            m = three(ps[:, 4 + nb, :], hTH[:, k, :], hTL[:, k, :], 2, slice(k * D + nb * N, k * D + nb * N + N),
                                      k == 0, k == 1)
                    m.then_inc(S("m_w2", l), 1)

                pe.wait_ge(sem("ctl_ready"), at("ctl_ready", l, 1))
                last = pe.value_load(ctl[0:1, 0:1], min_val=1, max_val=MAXB - 1)
                x_chunks(0)
                with pe.Fori(0, last) as b:
                    block_body(b, False)
                block_body(last, True)


def shape_constants():
    import numpy as np

    half = 16
    inv = (1.0 / (np.float32(10000.0) ** (np.arange(half, dtype=np.float32) * 2.0 / 32))).astype(np.float32)
    n = np.arange(NLT * P)
    ang = np.stack([(n // 64).astype(np.float32)[:, None] * inv, (n % 64).astype(np.float32)[:, None] * inv], 1)
    cos, sin = np.cos(ang), np.sin(ang)
    tab = np.zeros((P, NT, 2, 64), np.float32)
    tab[:, CTX, 0, :] = 1.0
    c = np.concatenate([cos, cos], -1).reshape(NLT, P, 64)
    s = np.concatenate([-sin, sin], -1).reshape(NLT, P, 64)
    tab[:, :NLT, 0, :] = c.transpose(1, 0, 2)
    tab[:, :NLT, 1, :] = s.transpose(1, 0, 2)
    pcon = np.zeros((P, 64), np.float32)
    pcon[:, 0:4] = [4, 3, 2, 1]
    pcon[:, 4:9] = np.arange(5) * 128
    pcon[:, 9:9 + LB] = np.arange(LB)
    pcon[:, 40] = np.arange(P) + 1
    pcon[:, 41:46] = np.arange(5) * 128
    pcon[:, 46:62] = 1.0
    return {
        "k_ident": np.eye(P, dtype=np.float32),
        "k_iota": np.tile(np.arange(P, dtype=np.float32), (P, 1)),
        "k_upper": np.triu(np.ones((P, P), np.float32), 1),
        "k_rope": tab,
        "k_pcon": pcon,
    }


_OUTS = [("y_prompt", (1, 128, 1024)), ("y_sample", (1, 512, 1024)),
         ("new_k", (1, 2, 128, 2, 64)), ("new_v", (1, 2, 128, 2, 64))]


def kernel(**inputs):
    import numpy as np
    import concourse.bacc as bacc
    from concourse.bass_utils import run_bass_kernel_spmd

    nc = bacc.Bacc("TRN2", target_bir_lowering=False, num_devices=1)
    arrays, I, O = {}, {}, {}
    for name, a in {**inputs, **shape_constants()}.items():
        a = np.ascontiguousarray(a)
        arrays[f"in_{name}"] = a
        I[name] = nc.dram_tensor(f"in_{name}", a.shape, mybir.dt.from_np(a.dtype), kind="ExternalInput").ap()
    for name, shape in _OUTS:
        O[name] = nc.dram_tensor(f"out_{name}", shape, F32, kind="ExternalOutput").ap()
    build(nc, I, O)
    r = run_bass_kernel_spmd(nc, [arrays], core_ids=[0])
    return tuple(r.results[0][f"out_{name}"] for name, _ in _OUTS)
```

```python
from contextlib import ExitStack

import concourse.bass as bass
from concourse import mybir

P = 128
D = 1024
DEPTH = 2
NT = 5
NLT = 4
CTX = 4
TOK = NT * P
KD = D // P
NH, NKV, HD = 8, 2, 64
D_IN = 2048
NG, NE, EPG = 4, 16, 4
F = 256
EPS = 1e-6
U = 2048
N = 512
RAWS = 4
HLS = 3
PAIRS = 2 * TOK
MINB = NE
MAXB = PAIRS // P + NE
LB = MAXB
NOROW = 8192
CACHE, CTXK = 4, 5
NKEY = 6

F32 = mybir.dt.float32
F32R = mybir.dt.float32r
BF16 = mybir.dt.bfloat16
I32 = mybir.dt.int32
U32 = mybir.dt.uint32
ALU = mybir.AluOpType
ACT = mybir.ActivationFunctionType
X = mybir.AxisListType.X

STREAM, START = [("ada", 0, n) for n in range(8)], [0]
for _l in range(DEPTH):
    STREAM += [("w", _l, n) for n in range(8)] + [("ada", _l, n) for n in range(8, 24)] + [("w", _l, n) for n in range(8, 12)]
    if _l + 1 < DEPTH:
        STREAM += [("ada", _l + 1, n) for n in range(8)]
    START.append(len(STREAM))
POS = {u: i for i, u in enumerate(STREAM)}


PER_LAYER = {
    "ada_read": 24, "piece_done": 12, "piece_out": 8 * 16,
    "norm2_row": 16, "a2_row": 2, "params_loaded": 15 * 16, "taps_loaded": 32, "tabs": 6, "modc_part": 3, "modc_psum": 1, "a1_ready": 1,
    "ss1": NT, "rstd1": NT, "xr_ready": NT, "hT_psum": KD, "h_full": 2 * KD, "h_hi": KD, "h_lo": KD,
    "w_hi": 12, "w_lo": 12, "w_used": 6, "proj": 4 * NT, "proj_read": 4 * NT, "zpn_zero": 2,
    "sq": 2 * NT, "ssqk": 2 * NT, "rqk": 2 * NT, "kv_raw": NT, "sv_raw": NT, "q_final": NT, "k_final": NT,
    "z_done": NT, "shifted": 64, "conv_done": 1, "front_used": 1, "sgT_psum": 1, "sgT_ready": 1, "sgu_psum": 4, "sgu_done": 4,
    "v_hi": NKV, "v_lo": NKV, "k_hi": NKV, "k_lo": NKV, "kT_psum": NKEY, "kk": NKEY,
    "q_hi": NT, "q_lo": NT, "qT_psum": 2 * NT, "qT": 2 * NT, "scores": NT * NH, "nmax": NT * NH, "prob": NT * NH,
    "pT_psum": NT * NH, "pT_hi": NT * NH, "pT_lo": NT * NH, "pv": NT * NH, "o_low": 2 * NT, "o_read": 2 * NT,
    "attn_done": 2 * NT, "ss3": 3 * NT, "rstd3": NT, "mrg_ready": 3 * NT, "mT_psum": KD, "mT_hi": 2 * KD, "mT_lo": 2 * KD,
    "gate1_row": 32, "scale2_row": 32, "shift2_row": 32, "gate2_row": 32, "oproj_psum": 2 * NT, "oproj": 2 * NT,
    "x_attn": 2 * NT, "ss2": NT, "rstd2": NT, "h2": NT, "h2T_psum": NT, "h2T": NT, "h2_stored0": 48, "h2_stored1": 32, "logits": NT,
    "rt_exp_in": 2, "rt_exp": 2, "choice": 1, "counts_psum": 1, "lists": 1, "list_psum": 1, "xg_zero": 1, "ctl_ready": 1,
    "y_scaled": NT, "moe_split_done": 1, "x_moe": NT,
}


def f32(ap):
    return ap.bitcast(F32)


def build(nc, I, O):
    with ExitStack() as ctx:
        def sb(name, shape, dt=F32):
            return ctx.enter_context(nc.sbuf_tensor(name, shape, dt))

        sems = {}

        def sem(name):
            if name not in sems:
                sems[name] = ctx.enter_context(nc.semaphore(name))
            return sems[name]

        modrow = [nc.dram_tensor(f"modrow{l}", [2, 6 * D], F32, kind="Internal").ap() for l in range(DEPTH)]
        h2s = [nc.dram_tensor(f"h2s{l}", [TOK, D], F32, kind="Internal").ap() for l in range(DEPTH)]
        ys = nc.dram_tensor("ys", [MAXB * P, D], F32, kind="Internal").ap()

        x = sb("x", [P, NT, D])
        actH = sb("actH", [P, KD * TOK], F32R)
        actL = sb("actL", [P, KD * TOK], F32R)
        raw = sb("raw", [P, RAWS, U])
        wH = sb("wH", [P, HLS, U], F32R)
        wL = sb("wL", [P, HLS, U], F32R)
        pool = sb("pool", [P, 13312])
        ident = sb("ident", [P, P])
        iota = sb("iota", [P, P])
        ones = sb("ones", [P, P], BF16)
        upper = sb("upper", [P, P], BF16)
        tabs = sb("tabs", [P, NT, 2, 2, HD])
        misc = sb("misc", [P, 1280])
        cw = misc[:, 0:768].rearrange("p (w n) -> p w n", w=3)
        sgw = misc[:, 768:1280].rearrange("p (g q) -> p g q", g=4)
        piece, bpiece = misc[0:2, 0:N], misc[0:2, N:2 * N]
        sgb = sb("sgb", [P, 4])
        rw = sb("rw", [P, KD, NG + NE])
        rb = sb("rb", [P, NG + NE])
        gains = sb("gains", [P, 2, HD])
        cols = sb("cols", [P, (1 + DEPTH) * KD])
        csil = sb("csil", [P, KD, 2])
        modc = sb("modc", [P, 16, 2])
        stat = sb("stat", [P, 64])
        nhalf = sb("nhalf", [P, 16])
        rsum = sb("rsum", [P, 2 * NH])
        nmax = sb("nmax", [P, 4])
        rinv = sb("rinv", [P, NH])
        pcon = sb("pcon", [P, 64])
        gate = sb("gate", [P, 2, NT])
        slot = sb("slot", [P, 2 * NT], U32)
        idxs = sb("idxs", [P, LB], U32)
        idxc = sb("idxc", [P, 2], U32)
        ctl = sb("ctl", [1, 32], I32)
        ps = ctx.enter_context(nc.psum_tensor("ps", [P, 8, 512], F32))

        actHk = actH[:, :].rearrange("p (k t) -> p k t", k=KD)
        actLk = actL[:, :].rearrange("p (k t) -> p k t", k=KD)
        kk = actH[:, 0:3072].rearrange("p (c n) -> p c n", c=4)
        pTH = actH[:, 3072:4352].rearrange("p (b n) -> p b n", b=2)
        pTL = actL[:, 3072:4352].rearrange("p (b n) -> p b n", b=2)
        vv = [t[:, 4352:5120].rearrange("p (j n) -> p j n", j=NKEY) for t in (actH, actL)]
        qT = actL[:, 0:2048].rearrange("p (b h n) -> p b h n", b=2, h=NH)
        qhl = actL[:, 2048:3072].rearrange("p (h s d) -> p h s d", h=NH, s=2)
        kdup = [w[:, 2, 0:1536].rearrange("p (j v s d) -> p j v s d", j=NKEY, v=NKV, s=2) for w in (wH, wL)]
        xTH = actH[:, 0:1024].rearrange("p (k n) -> p k n", k=KD)
        xTL = actL[:, 0:1024].rearrange("p (k n) -> p k n", k=KD)
        hTH = actH[:, 1024:1280].rearrange("p (k n) -> p k n", k=2)
        hTL = actL[:, 1024:1280].rearrange("p (k n) -> p k n", k=2)

        mrg = pool[:, 0:5120].rearrange("p (t n) -> p t n", t=NT)
        aux = pool[:, 5120:10240]
        pbuf = pool[:, 10240:11776]
        kv = pool[:, 11776:13312].rearrange("p (j n) -> p j n", j=NKEY)
        bias0 = pool[0:2, 5120:5120 + 4 * N]
        y1 = [pool[:, c:c + D] for c in (2048, 0, 4096, 7168, 9216)]
        y2 = [pool[:, c:c + D] for c in (3072, 1024, 10240, 8192, 11776)]
        xr = y1
        hf = pbuf[:, 0:1280].rearrange("p (b n) -> p b n", b=2)
        sv = aux[:, 0:1280].rearrange("p (t n) -> p t n", t=NT)
        z = aux[:, 1280:2560].rearrange("p (t n) -> p t n", t=NT)
        zp = aux[:, 2560:3840].rearrange("p (t n) -> p t n", t=NT)
        zn = aux[:, 3840:5120].rearrange("p (t n) -> p t n", t=NT)
        sgT = pbuf[:, 1024:1536].rearrange("p (g q) -> p g q", g=4)
        junk3 = pool[:, 11776:12288]
        prob = pbuf[:, 0:1280].rearrange("p (b n) -> p b n", b=2)
        grow = aux[:, 0:2048].rearrange("p (c n) -> p c n", c=2)
        arow = aux[:, 2048:4096].rearrange("p (c n) -> p c n", c=2)
        n2row = aux[:, 4096:5120]
        h2T = [r.rearrange("p (k n) -> p k n", k=KD) for r in (aux[:, 4096:5120], pool[:, 4096:5120])]
        srow = pool[:, 0:2048].rearrange("p (c n) -> p c n", c=2)
        h2b = pool[:, 2048:4096].rearrange("p (b n) -> p b n", b=2)
        otmp = pool[:, 10240:12288].rearrange("p (b n) -> p b n", b=4)
        junk2 = pool[:, 12288:13312]
        frow = tabs[:, :, :, :, :].rearrange("p t a b d -> p (t a b d)")[:, 0:D]
        xg = pool[:, 9216:11264].rearrange("p (b n) -> p b n", b=2)
        hid = pool[:, 11264:11776]
        yb = pool[:, 11776:12800]
        yo = (yb, pool[:, 7168:8192])
        rt = pool[:, 11264:13312]
        used = [0]

        def tmp(*shape, dt=F32):
            n = 1
            for s_ in shape:
                n *= s_
            if dt == BF16:
                n //= 2
            v = rt[:, used[0]:used[0] + n]
            used[0] += n
            v = v if dt == F32 else v.bitcast(dt)
            names = " ".join("abcd"[:len(shape)])
            return v if len(shape) == 1 else v.rearrange(f"p ({names}) -> p {names}", **dict(zip("abcd", shape)))

        pr2 = tmp(160)
        ex, d_ = tmp(NT, 4), tmp(NT)
        lg, gm, sm, eq = tmp(NT, NG + NE), tmp(NT), tmp(NT), tmp(NT, 4)
        og, o1, o2, es, e2 = (tmp(NT, 4) for _ in range(5))
        em1, em2, pg = tmp(NT), tmp(NT), tmp(NT)
        pr = tmp(NT, 4, 4)
        M = tmp(2, NT, NE)
        Mb = tmp(NT, NE, dt=BF16)
        pos, cnt, cmp5 = tmp(NT * NE), tmp(NE), tmp(NE, 5)
        nb_, incl, base = tmp(NE), tmp(NE), tmp(NE)
        q, eb, qd = tmp(10), tmp(10), tmp(10)
        oneb = tmp(10, LB, dt=BF16)
        tl = tmp(10, 2, LB, dt=BF16)
        eb26 = tmp(32)
        one_r = pool[:, 10240:10880].bitcast(BF16).rearrange("p (c n) -> p c n", c=10)

        s_raw = [sem(f"raw_loaded{i}") for i in range(RAWS)]
        flat = ps[:, :, :].rearrange("p b n -> p (b n)")
        ORDER = (CTX, 0, 1, 2, 3)
        two, one = (0, 0, 3, 3, 2, 3, 3, 2), (0, 0, 1, 1, 1, 2, 1, 2)
        ADA_AT = two + one + two + one + (2,) * NH
        PIECE_AT = [u for u in range(NT * NH) if ADA_AT[u] and sum(ADA_AT[:u + 1]) % KD == 0]
        W_AT = {36: 8}

        def ada_bank(l, g):
            return 7 if g >= 4 else 6 if l else 5 + g % 2

        block = ctx.enter_context(nc.Block())

        def at(name, l, n):
            return l * PER_LAYER[name] + n

        def unit_used(eng, i):
            kind, l, n = STREAM[i]
            if kind == "ada":
                eng.wait_ge(sem("ada_read"), at("ada_read", l, n + 1))
            else:
                eng.wait_ge(sem("w_lo"), at("w_lo", l, n + 1))

        def unit_loaded(eng, kind, l, n):
            i = POS[kind, l, n]
            eng.wait_ge(s_raw[i % RAWS], 16 * (i // RAWS + 1))

        def w_read(eng, l, i):
            if i % 2 == 0:
                eng.wait_ge(sem("w_used"), at("w_used", l, i // 2 + 1))
            elif i < 8:
                eng.wait_ge(sem("proj"), at("proj", l, NT * (i // 2 + 1)))
            else:
                eng.wait_ge(sem("oproj_psum"), at("oproj_psum", l, NT * (i // 2 - 3)))

        @block.sync
        def _(sp):
            sp.dma_start(csil[:, :, 0], I["c"].rearrange("a (k p) -> p (a k)", p=P),
                         allow_slow_non_contiguous=True).then_inc(sem("c_loaded"), 16)
            sp.dma_start(csil[:, :, 1], I["c_ctx"].rearrange("(k p) -> p k", p=P),
                         allow_slow_non_contiguous=True).then_inc(sem("c_loaded"), 16)
            first = 0

            def row(ap):
                return ap.partition_broadcast(P)

            def load_params(l):
                lp = sem("params_loaded")
                for qk in range(2):
                    sp.dma_start(tabs[:, :, qk, :, :], I["k_rope"]).then_inc(lp, 16)
                sp.dma_start(gains[:, 0, :], row(I["q_norm"][l])).then_inc(lp, 16)
                sp.dma_start(gains[:, 1, :], row(I["k_norm"][l])).then_inc(lp, 16)
                sp.dma_start(cols[:, 0:KD], I["out_norm"][l].rearrange("(k p) -> p k", p=P),
                             allow_slow_non_contiguous=True).then_inc(lp, 16)
                sp.dma_start(sgb[:, :], I["sgu_b"][l].rearrange("g p -> p g"),
                             allow_slow_non_contiguous=True).then_inc(lp, 16)
                sp.dma_start(rw[:, :, 0:NG], I["router_g_w"][l].rearrange("(k p) g -> p k g", p=P)).then_inc(lp, 16)
                for g in range(NG):
                    sp.dma_start(rw[:, :, NG + EPG * g:NG + EPG * (g + 1)],
                                 I["router_e_w"][l, g].rearrange("(k p) e -> p k e", p=P)).then_inc(lp, 16)
                sp.dma_start(rb[:, 0:NG], row(I["router_g_b"][l])).then_inc(lp, 16)
                sp.dma_start(rb[:, NG:], row(I["router_e_b"][l].rearrange("g e -> (g e)"))).then_inc(lp, 16)
                sp.dma_start(kv[:, CACHE, 0:P], I["cache_k"][0, l].rearrange("m h d -> m (h d)")).then_inc(lp, 16)
                sp.dma_start(kv[:, CACHE, P:], I["cache_v"][0, l].rearrange("m h d -> m (h d)")).then_inc(lp, 16)

            def load_taps(l):
                sp.wait_ge(sem("modc_psum"), at("modc_psum", l, 1))
                sp.wait_ge(sem("piece_done"), at("piece_done", l, 4))
                sp.dma_start(cw.rearrange("p w n -> p (w n)"), row(I["conv_w"][l].rearrange("w n -> (w n)"))
                             ).then_inc(sem("taps_loaded"), 16)
                sp.dma_start(sgw, I["sgu_w"][l].rearrange("g p q -> p g q")).then_inc(sem("taps_loaded"), 16)

            for l in range(DEPTH):
                for i in range(START[l], START[l + 1]):
                    kind, ll, n = STREAM[i]
                    if i == START[l] + (20 if l == 0 else 12):
                        sp.wait_ge(sem("z_done"), at("z_done", l, NT))
                        sp.wait_ge(sem("zpn_zero"), at("zpn_zero", l, 2))
                        sh = sem("shifted")
                        sp.dma_start(zp[1:P, :, :], z[0:P - 1, :, :]).then_inc(sh, 16)
                        sp.dma_start(zp[0:1, 1:NLT, :], z[P - 1:P, 0:NLT - 1, :]).then_inc(sh, 16)
                        sp.dma_start(zn[0:P - 1, :, :], z[1:P, :, :]).then_inc(sh, 16)
                        sp.dma_start(zn[P - 1:P, 0:NLT - 1, :], z[0:1, 1:NLT, :]).then_inc(sh, 16)
                        sp.wait_ge(sem("k_final"), at("k_final", l, NT))
                        sp.dma_start(O["new_k"][0, l].rearrange("s h d -> s (h d)"), kv[:, CTXK, 0:P]).then_inc(sem("out_done"), 16)
                        sp.dma_start(O["new_v"][0, l].rearrange("s h d -> s (h d)"), kv[:, CTXK, P:]).then_inc(sem("out_done"), 16)
                    if l > 0 and i < START[l] + HLS:
                        sp.wait_ge(sem("moe_split_done"), at("moe_split_done", l - 1, 1))
                        sp.wait_ge(sem(f"y_in{NT - 2}"), 32 * l)
                    elif i >= RAWS:
                        unit_used(sp, i - RAWS)
                    if 3 <= i < 3 + NT:
                        t = i - 3
                        src = I["x_sample"][0, t * P:(t + 1) * P, :] if t < CTX else I["x_prompt"][0]
                        sp.dma_start(x[:, t, :], src).then_inc(sem(f"x_loaded{t}"), 16)
                    if i == 12:
                        load_params(0)
                        load_taps(0)
                    if i == 14:
                        sp.wait_ge(sem("x_loaded0"), 16)
                        for j in range(MINB, MAXB):
                            sp.dma_start(ys[j * P:(j + 1) * P, :], x[:, 0, :]).then_inc(sem("ys_filled"), 16)
                    k0, n0 = (n % 2) * 4, (n // 2) * N
                    if kind == "ada":
                        src = I["w_ada"][ll, k0 * P:(k0 + 4) * P, n0:n0 + N]
                    elif n < 8:
                        src = I["w_in"][l, k0 * P:(k0 + 4) * P, n0:n0 + N]
                    else:
                        n0 -= 4 * N
                        src = I["w_out"][l, k0 * P:(k0 + 4) * P, n0:n0 + N]
                    sp.dma_start(raw[:, i % RAWS, :].rearrange("p (k n) -> p k n", k=4),
                                 src.rearrange("(k p) n -> p k n", p=P)).then_inc(s_raw[i % RAWS], 16)

                w1, w3, w2 = I["moe_w1"][l], I["moe_w3"][l], I["moe_w2"][l]

                def expert(b):
                    return sp.value_load(ctl[0:1, bass.ds(b + 1, 1)], min_val=0, max_val=NE - 1)

                def load_w13(u, b, e):
                    if b is not None:
                        b = b + first if isinstance(b + first, int) else sp.snap(b + first, min_val=1, max_val=DEPTH * MAXB)
                        sp.wait_ge(sem(f"m_lo{u}"), b)
                    for j, w in enumerate((w1, w3)):
                        sp.dma_start(
                            raw[:, u, :].rearrange("p (k j f) -> p k j f", k=4, j=2)[:, :, j, :],
                            w[bass.ds(e, 1), u * N:(u + 1) * N, :].rearrange("a (k p) f -> p (a k) f", p=P)
                        ).then_inc(sem(f"m_raw{u}"), 16)

                def load_w2(b, e):
                    if b is not None:
                        b = b + first if isinstance(b + first, int) else sp.snap(b + first, min_val=1, max_val=DEPTH * MAXB)
                        sp.wait_ge(sem("m_lo2"), b)
                    sp.dma_start(raw[:, 2, :].rearrange("p (k n) -> p k n", k=2),
                                 w2[bass.ds(e, 1), :, :].rearrange("a (k p) n -> p (a k) n", p=P)
                                 ).then_inc(sem("m_raw2"), 16)

                def store_block(b, parity):
                    row = sp.snap(b * P, min_val=0, max_val=(MAXB - 1) * P)
                    count = sp.snap(b + first + 2, min_val=2, max_val=DEPTH * MAXB)
                    sp.wait_ge(sem("m_ya"), count)
                    sp.wait_ge(sem("m_yd"), count)
                    sp.dma_start(ys[bass.ds(row, P), :], yo[parity]).then_inc(sem(f"m_ys{parity}"), 16)

                unit_used(sp, START[l + 1] - RAWS)
                load_w13(0, None, 0)
                unit_used(sp, START[l + 1] - RAWS + 1)
                load_w13(1, None, 0)
                if l + 1 < DEPTH:
                    sp.wait_ge(sem("choice"), at("choice", l, 1))
                    load_params(l + 1)
                unit_used(sp, START[l + 1] - RAWS + 2)
                load_w2(None, 0)
                sp.wait_ge(sem("ctl_ready"), at("ctl_ready", l, 1))
                if l == 0:
                    sp.wait_ge(sem("ys_filled"), 16 * (MAXB - MINB))
                h = sp.value_load(ctl[0:1, 0:1], min_val=MINB // 2 - 2, max_val=MAXB // 2 - 2) + 1
                e = sp.value_load(ctl[0:1, 2:3], min_val=0, max_val=NE - 1)
                e2 = sp.value_load(ctl[0:1, 3:4], min_val=0, max_val=NE - 1)
                load_w13(0, 1, e)
                load_w13(1, 1, e)
                load_w13(0, 2, e2)
                with sp.Fori(0, h - 1) as pair:
                    for parity in range(2):
                        b = pair * 2 + 2 + parity
                        load_w2(b - 1, expert(b - 1))
                        load_w13(1, b, expert(b))
                        load_w13(0, b + 1, expert(b + 1))
                        store_block(b - 2, parity)
                load_w2(h * 2 - 1, expert(h * 2 - 1))
                load_w13(1, h * 2, expert(h * 2))
                load_w13(0, h * 2 + 1, expert(h * 2 + 1))
                store_block(h * 2 - 2, 0)
                load_w2(h * 2, expert(h * 2))
                load_w13(1, h * 2 + 1, expert(h * 2 + 1))
                store_block(h * 2 - 1, 1)
                load_w2(h * 2 + 1, expert(h * 2 + 1))
                if l + 1 < DEPTH:
                    load_taps(l + 1)
                store_block(h * 2, 0)
                store_block(h * 2 + 1, 1)
                first = first + h * 2 + 2
            for t in range(NT):
                sp.wait_ge(sem("y_final"), t + 1)
                dst = O["y_sample"][0, t * P:(t + 1) * P, :] if t < CTX else O["y_prompt"][0]
                sp.dma_start(dst, x[:, t, :]).then_inc(sem("y_out"), 16)
            sp.wait_ge(sem("y_out"), 16 * NT)

        @block.gpsimd
        def _(pl):
            pl.dma_start(ident[:, :], I["k_ident"]).then_inc(sem("ident_loaded"), 16)
            pl.dma_start(iota[:, :], I["k_iota"]).then_inc(sem("consts_loaded"), 16)
            pl.dma_start(pcon[:, :], I["k_pcon"]).then_inc(sem("consts_loaded"), 16)
            pl.dma_start(rt[:, 0:P], I["k_upper"]).then_inc(sem("consts_loaded"), 16)
            for l in range(DEPTH):
                pl.dma_start(cols[:, KD * (1 + l):KD * (2 + l)], I["norm1"][l].rearrange("(k p) -> p k", p=P),
                             allow_slow_non_contiguous=True).then_inc(sem("norm1_loaded"), 16)
            pl.dma_start(bias0, I["b_ada"][0, 0:4 * N].partition_broadcast(2)).then_inc(sem("bias0_in"), 16)
            pl.memset(nhalf[:, :], -0.5).then_inc(sem("nhalf_set"), 1)
            pl.wait_ge(sem("nhalf_set"), 1)
            steps = [0]

            def link(ins):
                steps[0] += 1
                ins.then_inc(sem("pool_step"), 1)
                pl.wait_ge(sem("pool_step"), steps[0])

            def rstd(src, dst, n, width, ready, count, done):
                pl.wait_ge(ready, count)
                link(pl.tensor_scalar(dst, src, 1.0 / width, EPS, ALU.mult, ALU.add))
                pl.tensor_tensor(dst, dst, nhalf[:, 0:n], ALU.pow).then_inc(done, 1)

            def row(ap):
                return ap.partition_broadcast(P)

            def bias_in(l, g):
                if l or g > 4:
                    pl.wait_ge(sem("piece_done"), at("piece_done", l, g))
                pl.dma_start(bpiece, I["b_ada"][l, g * N:(g + 1) * N].partition_broadcast(2)).then_inc(sem("bias_in"), 16)

            def rstd1(l):
                for t in range(NT):
                    rstd(stat[:, t:t + 1], stat[:, 8 + t:9 + t], 1, D, sem("ss1"), at("ss1", l, t + 1), sem("rstd1"))

            rstd1(0)
            first = pairs = 0
            for l in range(DEPTH):
                pl.wait_ge(sem("hT_psum"), at("hT_psum", l, KD))
                pl.memset(zp[:, :, :], 0.0).then_inc(sem("zpn_zero"), 1)
                pl.memset(zn[:, :, :], 0.0).then_inc(sem("zpn_zero"), 1)
                for i in range(2 * NT):
                    n = NH if i < NT else NKV
                    c = 8 * (i % 2)
                    rstd(stat[:, 16 + c:16 + c + n], stat[:, 32 + c:32 + c + n], n, HD, sem("ssqk"), at("ssqk", l, i + 1), sem("rqk"))
                pl.wait_ge(sem("shifted"), at("shifted", l, 64))
                pl.wait_ge(sem("taps_loaded"), at("taps_loaded", l, 32))
                tap = lambda w: cw[:, w, :].unsqueeze(1).to_broadcast([P, NT, 256])
                link(pl.tensor_tensor(zp[:, :, :], zp[:, :, :], tap(0), ALU.mult))
                link(pl.tensor_tensor(z[:, :, :], z[:, :, :], tap(1), ALU.mult))
                link(pl.tensor_tensor(zn[:, :, :], zn[:, :, :], tap(2), ALU.mult))
                pl.wait_ge(sem("sgT_psum"), at("sgT_psum", l, 1))
                bias_in(l, 4)
                link(pl.tensor_tensor(z[:, :, :], z[:, :, :], zp[:, :, :], ALU.add))
                link(pl.tensor_tensor(z[:, :, :], z[:, :, :], zn[:, :, :], ALU.add))
                pl.tensor_tensor(mrg[:, :, 768:], mrg[:, :, 768:], z[:, :, :], ALU.mult).then_inc(sem("conv_done"), 1)
                pl.wait_ge(sem("conv_done"), at("conv_done", l, 1))
                pl.wait_ge(sem("sgu_done"), at("sgu_done", l, 4))

                def branch_stats(t):
                    pl.wait_ge(sem("ss3"), at("ss3", l, 3 * t + 3))
                    c = 32 + 3 * t
                    link(pl.tensor_scalar(stat[:, c:c + 1], stat[:, c:c + 1], 1.0 / 512, EPS, ALU.mult, ALU.add))
                    link(pl.tensor_scalar(stat[:, c + 1:c + 3], stat[:, c + 1:c + 3], 1.0 / 256, EPS, ALU.mult, ALU.add))
                    pl.tensor_tensor(stat[:, c + 16:c + 19], stat[:, c:c + 3], nhalf[:, 0:3], ALU.pow).then_inc(sem("rstd3"), 1)

                stats = 0
                for g in range(4, 12):
                    if g > 4:
                        bias_in(l, g)
                    while stats < NT - 1 and PIECE_AT[g - 4] >= NH * (stats + 1) + 3:
                        branch_stats(stats)
                        stats += 1
                    pl.wait_ge(sem("piece_done"), at("piece_done", l, g + 1))
                    pl.dma_start(modrow[l][:, g * N:(g + 1) * N], piece).then_inc(sem("piece_out"), 16)
                for t in range(stats, NT):
                    branch_stats(t)
                pl.dma_start(n2row, row(I["norm2"][l])).then_inc(sem("norm2_row"), 16)
                pl.wait_ge(sem("piece_out"), at("piece_out", l, 128))
                for c in range(2):
                    pl.dma_start(grow[:, c, :], row(modrow[l][c, 2 * D:3 * D])).then_inc(sem("gate1_row"), 16)
                    pl.dma_start(arow[:, c, :], row(modrow[l][c, 4 * D:5 * D])).then_inc(sem("scale2_row"), 16)
                pl.wait_ge(sem("mT_psum"), at("mT_psum", l, KD))
                for c in range(2):
                    pl.dma_start(srow[:, c, :], row(modrow[l][c, 3 * D:4 * D])).then_inc(sem("shift2_row"), 16)
                if l == DEPTH - 1:
                    pl.dma_start(frow, row(I["final_norm"])).then_inc(sem("final_row"), 16)
                if l + 1 < DEPTH:
                    bias_in(l + 1, 0)
                for i in range(2 * NT):
                    nb, t = divmod(i, NT)
                    xs = x[:, t, nb * N:(nb + 1) * N]
                    pl.wait_ge(sem("oproj"), at("oproj", l, i + 1))
                    pl.tensor_tensor(xs, xs, otmp[:, i % 4, :], ALU.add).then_inc(sem("x_attn"), 1)
                    for t in ([t - 1] if nb and t else []) + ([NT - 1] if i == 2 * NT - 1 else []):
                        rstd(stat[:, t:t + 1], stat[:, 8 + t:9 + t], 1, D, sem("ss2"), at("ss2", l, t + 1), sem("rstd2"))
                if l + 1 < DEPTH:
                    bias_in(l + 1, 1)
                for c in range(2):
                    pl.dma_start(grow[:, c, :], row(modrow[l][c, 5 * D:6 * D])).then_inc(sem("gate2_row"), 16)
                if l + 1 < DEPTH:
                    bias_in(l + 1, 2)
                    bias_in(l + 1, 3)

                pl.wait_ge(sem("list_psum"), at("list_psum", l, 1))
                pl.memset(xg[:, 1, :], 0.0).then_inc(sem("xg_zero"), 1)
                pl.wait_ge(sem("xg_zero"), at("xg_zero", l, 1))

                def take_idx(b, parity):
                    pl.tensor_copy(idxc[:, parity:parity + 1], idxs[:, bass.ds(b, 1)]).then_inc(sem("m_idx"), 1)
                    pl.wait_ge(sem("m_idx"), b + first + 1)
                    pl.sem_inc(sem("pool_passed"), 1)

                def gather(parity):
                    pl.indirect_dma_start(xg[:, parity, :], None, h2s[l], bass.IndirectOffsetOnAxis(idxc[:, parity:parity + 1], 0),
                                          bounds_check=TOK - 1, oob_is_err=False).then_inc(sem(f"m_g{parity}"), 16)

                pl.wait_ge(sem("ctl_ready"), at("ctl_ready", l, 1))
                for p_ in range(2):
                    pl.wait_ge(sem(f"h2_stored{p_}"), at(f"h2_stored{p_}", l + 1, 0))
                h = pl.value_load(ctl[0:1, 0:1], min_val=MINB // 2 - 2, max_val=MAXB // 2 - 2) + 1
                for parity in range(2):
                    take_idx(parity, parity)
                    gather(parity)
                with pl.Fori(0, h) as pair:
                    for parity in range(2):
                        b = pair * 2 + parity
                        pl.wait_ge(sem(f"m_g{parity}"), (pair + pairs) * 16 + 16)
                        pl.sem_inc(sem("pool_passed"), 1)
                        take_idx(b + 2, parity)
                        pl.wait_ge(sem("m_tx"), (b + first) * 2 + 2)
                        pl.sem_inc(sem("pool_passed"), 1)
                        gather(parity)
                first, pairs = first + h * 2 + 2, pairs + h + 1
                for parity in range(2):
                    pl.wait_ge(sem(f"m_ys{parity}"), pairs * 16 + 16)
                    pl.sem_inc(sem("pool_passed"), 1)
                for t in range(NT):
                    for c, y in enumerate((y1[t], y2[t])):
                        pl.indirect_dma_start(y, None, ys, bass.IndirectOffsetOnAxis(slot[:, c * NT + t:c * NT + t + 1], 0)
                                              ).then_inc(sem(f"y_in{t}"), 16)
                rstd1(l + 1)

        @block.scalar
        def _(act):
            steps = [0]

            def link(ins):
                steps[0] += 1
                ins.then_inc(sem("act_step"), 1)
                act.wait_ge(sem("act_step"), steps[0])

            act.wait_ge(sem("c_loaded"), 32)
            act.activation(csil[:, :, :], csil[:, :, :], ACT.Silu).then_inc(sem("c_silu"), 1)

            def norm1_square(l, t):
                act.activation(y2[t], x[:, t, :], ACT.Square, accum_out=stat[:, t:t + 1]).then_inc(sem("ss1"), 1)

            def norm1_scale(l, t):
                if l < DEPTH:
                    act.wait_ge(sem("rstd1"), at("rstd1", l, t + 1))
                    act.activation(xr[t], x[:, t, :], ACT.Identity, scale=stat[:, 8 + t:9 + t]).then_inc(sem("xr_ready"), 1)

            for t in range(NT):
                act.wait_ge(sem(f"x_loaded{t}"), 16)
                norm1_square(0, t)
            for t in range(NT):
                norm1_scale(0, t)
            first = pairs = 0
            for l in range(DEPTH):
                def split_hi(i):
                    unit_loaded(act, "w", l, i)
                    if i >= HLS:
                        w_read(act, l, i - HLS)
                    act.activation(wH[:, i % HLS, :], raw[:, POS["w", l, i] % RAWS, :], ACT.Copy).then_inc(sem("w_hi"), 1)

                split_hi(0)
                for k in range(KD):
                    act.wait_ge(sem("hT_psum"), at("hT_psum", l, k + 1))
                    if k == 0:
                        act.wait_ge(sem("a1_ready"), at("a1_ready", l, 1))
                    if k >= 2:
                        act.wait_ge(sem("h_lo"), at("h_lo", l, k - 1))
                    act.activation(hf[:, k % 2, 0:512], ps[:, 5 + 2 * (k % 2), :], ACT.Identity,
                                   bias=modc[:, k, 0:1], scale=modc[:, KD + k, 0:1]).then_inc(sem("h_full"), 1)
                    act.activation(hf[:, k % 2, 512:640], ps[:, 6, 0:P], ACT.Identity,
                                   bias=modc[:, k, 1:2], scale=modc[:, KD + k, 1:2]).then_inc(sem("h_full"), 1)
                    act.wait_ge(sem("h_full"), at("h_full", l, 2 * k + 2))
                    act.activation(actHk[:, k, :], hf[:, k % 2, :], ACT.Copy).then_inc(sem("h_hi"), 1)
                    if k == 2:
                        split_hi(1)
                split_hi(2)
                def q_hi(t):
                    act.wait_ge(sem("q_final"), at("q_final", l, ORDER[t] + 1))
                    if t:
                        act.wait_ge(sem("qT_psum"), at("qT_psum", l, 2 * t))
                    act.activation(qhl[:, :, 0, :], mrg[:, ORDER[t], 0:512].rearrange("p (h d) -> p h d", h=NH), ACT.Copy
                                   ).then_inc(sem("q_hi"), 1)

                def keys_out(j):
                    act.wait_ge(sem("kT_psum"), at("kT_psum", l, j + 1))
                    act.activation(kk[:, :, j * P:(j + 1) * P], ps[:, 4 + j % 2, :].rearrange("p (c n) -> p c n", c=4),
                                   ACT.Copy).then_inc(sem("kk"), 1)

                act.wait_ge(sem("params_loaded"), at("params_loaded", l, 15 * 16))
                done = 3
                for gi in range(4 * NT):
                    nb, t = divmod(gi, NT)
                    bank = ps[:, gi % 8, :]
                    if t == 0:
                        while done < min(8, 2 * nb + 4):
                            split_hi(done)
                            done += 1
                    if nb == 3 and t == 0:
                        act.wait_ge(sem("k_final"), at("k_final", l, NT))
                        w_read(act, l, 5)
                        kf = kv[:, :, 0:P].rearrange("p j (v d) -> p j v d", v=NKV)
                        for v in range(NKV):
                            act.activation(kdup[0][:, :, v, :, :], kf[:, :, v, :].unsqueeze(2).to_broadcast([P, NKEY, 2, HD]), ACT.Copy
                                           ).then_inc(sem("k_hi"), 1)
                        act.wait_ge(sem("front_used"), at("front_used", l, 1))
                        q_hi(0)
                        act.wait_ge(sem("sgT_psum"), at("sgT_psum", l, 1))
                        act.activation(sgT[:, :, :].rearrange("p g q -> p (g q)"), ps[:, 6, :], ACT.Copy).then_inc(sem("sgT_ready"), 1)
                        keys_out(0)
                        keys_out(1)
                    act.wait_ge(sem("proj"), at("proj", l, gi + 1))
                    free = sem("proj_read")
                    if nb == 0:
                        act.activation(mrg[:, t, 512:1024], bank, ACT.Square).then_inc(sem("sq"), 1)
                        act.activation(mrg[:, t, 0:512], bank, ACT.Copy).then_inc(free, 1)
                    elif nb == 1:
                        j = t if t < CTX else CTXK
                        act.wait_ge(sem("ssqk"), at("ssqk", l, t + 1))
                        act.activation(mrg[:, t, 768:768 + P], bank[:, 0:P], ACT.Square).then_inc(sem("sq"), 1)
                        act.activation(kv[:, j, :], bank[:, 0:256], ACT.Copy).then_inc(sem("kv_raw"), 1)
                        act.activation(mrg[:, t, 512:768], bank[:, 256:512], ACT.Copy).then_inc(free, 1)
                    elif nb == 2:
                        act.wait_ge(sem("ssqk"), at("ssqk", l, NT + t + 1))
                        act.activation(sv[:, t, :], bank[:, 0:256], ACT.Copy).then_inc(sem("sv_raw"), 1)
                        act.activation(mrg[:, t, 768:1024], bank[:, 256:512], ACT.Copy).then_inc(free, 1)
                    else:
                        act.activation(z[:, t, :], bank[:, 0:256], ACT.Copy).then_inc(free, 1)
                for v in range(NKV):
                    act.activation(vv[v][:, :, 0:HD], kv[:, :, P + HD * v:P + HD * (v + 1)], ACT.Copy).then_inc(sem("v_hi"), 1)
                for j in range(2, NKEY):
                    keys_out(j)

                def q_out(t, r):
                    act.wait_ge(sem("qT_psum"), at("qT_psum", l, 2 * t + r + 1))
                    act.activation(qT[:, t % 2, 4 * r:4 * r + 4, :].rearrange("p h n -> p (h n)"), ps[:, 7, :], ACT.Copy
                                   ).then_inc(sem("qT"), 1)

                def o_low(g):
                    t, r = divmod(g, 2)
                    act.wait_ge(sem("pv"), at("pv", l, 4 * g + 4))
                    act.activation(mrg[:, ORDER[t], 256 * r:256 * r + 256].rearrange("p (h d) -> p h d", h=4),
                                   ps[:, 6, :].rearrange("p (h s d) -> p h s d", h=4, s=2)[:, :, 1, :], ACT.Copy
                                   ).then_inc(sem("o_low"), 1)

                act.wait_ge(sem("kT_psum"), at("kT_psum", l, NKEY))
                def branch_squares(t):
                    act.wait_ge(sem("attn_done"), at("attn_done", l, 2 * t + 2))
                    if t == 0:
                        act.wait_ge(sem("conv_done"), at("conv_done", l, 1))
                        act.wait_ge(sem("sgu_done"), at("sgu_done", l, 4))
                    for j, (a, b) in enumerate(((0, 512), (512, 768), (768, 1024))):
                        if 3 * t + j:
                            act.wait_ge(sem("ss3"), at("ss3", l, 3 * t + j))
                        act.activation(junk3[:, 0:b - a], mrg[:, ORDER[t], a:b], ACT.Square,
                                       accum_out=stat[:, 32 + 3 * t + j:33 + 3 * t + j]).then_inc(sem("ss3"), 1)

                q_out(0, 0)
                q_out(0, 1)
                q_hi(1)
                for u in range(NT * NH + 1):
                    if u >= 1:
                        v = u - 1
                        keys = 5 * P if v >= NH else P
                        act.wait_ge(sem("pT_psum"), at("pT_psum", l, v + 1))
                        if v >= 2:
                            act.wait_ge(sem("pv"), at("pv", l, v - 1))
                        act.activation(pTH[:, v % 2, 0:keys], flat[:, 4 * N:4 * N + keys],
                                       ACT.Copy).then_inc(sem("pT_hi"), 1)
                    if u < NT * NH:
                        t, h = divmod(u, NH)
                        keys = 5 * P if t else P
                        act.wait_ge(sem("nmax"), at("nmax", l, u + 1))
                        if u >= 2:
                            act.wait_ge(sem("pT_psum"), at("pT_psum", l, u - 1))
                        act.activation(prob[:, u % 2, 0:keys], flat[:, 2 * N * (u % 2):2 * N * (u % 2) + keys], ACT.Exp, bias=nmax[:, u % 2:u % 2 + 1],
                            accum_out=rsum[:, u % 16:u % 16 + 1]).then_inc(sem("prob"), 1)
                    if u >= 2 and (u - 2) % 4 == 3:
                        o_low((u - 2) // 4)
                    if u in W_AT:
                        split_hi(W_AT[u])
                    if u == NLT * NH + 3:
                        branch_squares(NLT - 1)
                    if u < NLT * NH:
                        t, h = divmod(u, NH)
                        if h < 2:
                            q_out(t + 1, h)
                        if h == 3 and t:
                            branch_squares(t - 1)
                        if h == 2 and t + 2 < NT:
                            q_hi(t + 2)
                o_low(2 * NT - 1)
                branch_squares(NT - 1)
                for k in range(KD):
                    act.wait_ge(sem("mT_psum"), at("mT_psum", l, k + 1))
                    on = cols[:, k:k + 1]
                    act.activation(actHk[:, k, 0:512], ps[:, 5 + 2 * (k % 2), :], ACT.Identity, scale=on).then_inc(sem("mT_hi"), 1)
                    act.activation(actHk[:, k, 512:640], ps[:, 6, 0:P], ACT.Identity, scale=on).then_inc(sem("mT_hi"), 1)
                    if k == 1:
                        split_hi(9)
                for i in range(10, 12):
                    split_hi(i)
                act.wait_ge(sem("out_done"), 32 * (l + 1))
                for t in range(NT):
                    act.wait_ge(sem("x_attn"), at("x_attn", l, NT + t + 1))
                    if t:
                        act.wait_ge(sem("ss2"), at("ss2", l, t))
                    act.activation(junk2, x[:, t, :], ACT.Square, accum_out=stat[:, t:t + 1]).then_inc(sem("ss2"), 1)
                for t in range(NT):
                    act.wait_ge(sem("h2T_psum"), at("h2T_psum", l, t + 1))
                    act.dma_start(h2s[l][t * P:(t + 1) * P, :], h2b[:, t % 2, :]).then_inc(sem(f"h2_stored{t % 2}"), 16)
                    if t >= 2:
                        act.wait_ge(sem("logits"), at("logits", l, t - 1))
                    b0 = 2 * (t % 2)
                    act.activation(h2T[t % 2].rearrange("p k n -> p (k n)"), ps[:, b0:b0 + 2, :].rearrange("p b n -> p (b n)"),
                                   ACT.Copy).then_inc(sem("h2T"), 1)
                def m_split(i, b):
                    act.wait_ge(sem(f"m_raw{i}"), (b + 1) * (32 if i < 2 else 16))
                    act.activation(wH[:, i, :], raw[:, i, :], ACT.Copy).then_inc(sem(f"m_hi{i}"), 1)

                w_read(act, l, 11)
                for i in range(2):
                    act.wait_ge(sem("rt_exp_in"), at("rt_exp_in", l, i + 1))
                    e_ = (ex, d_)[i]
                    act.activation(e_, e_, ACT.Exp).then_inc(sem("rt_exp"), 1)
                m_split(0, first)
                m_split(1, first)
                act.activation(nmax[:, 2:4], nmax[:, 0:2], ACT.Silu)

                def x_hi(h, b):
                    act.wait_ge(sem("m_tx"), b * 2 + h + 1)
                    act.activation(actH[:, N * h:N * h + N], ps[:, 1 + h, :], ACT.Copy).then_inc(sem("m_xh"), 1)

                def block_body(b, parity, pair, left):
                    if left >= 1:
                        x_hi(0, b + 1)
                    m_split(2, b)
                    act.wait_ge(sem("m_w13"), b * 2 + 2)
                    act.activation(hid[:, 0:F], ps[:, 0, 0:F], ACT.Silu).then_inc(sem("m_sg"), 1)
                    act.wait_ge(sem("m_th"), b + 1)
                    act.activation(hTH.rearrange("p k n -> p (k n)"), ps[:, 3, 0:F], ACT.Copy).then_inc(sem("m_hh"), 1)
                    if left >= 1:
                        m_split(1, b + 1)
                        x_hi(1, b + 1)
                    if left >= 2:
                        act.wait_ge(sem("m_w13"), b * 2 + 3)
                        m_split(0, b + 2)
                    act.wait_ge(sem("m_w2"), b + 1)
                    act.wait_ge(sem(f"m_ys{parity}"), pair * 16 + 16)
                    act.activation(yo[parity][:, 0:N], ps[:, 4, :], ACT.Copy).then_inc(sem("m_ya"), 1)

                act.wait_ge(sem("ctl_ready"), at("ctl_ready", l, 1))
                h = act.value_load(ctl[0:1, 0:1], min_val=MINB // 2 - 2, max_val=MAXB // 2 - 2) + 1
                if l == 0:
                    act.sem_inc(sem("m_ya"), 1)
                    act.sem_inc(sem("m_ys0"), 16)
                x_hi(0, first)
                x_hi(1, first)
                act.wait_ge(sem("m_w13"), first * 2 + 1)
                m_split(0, first + 1)
                with act.Fori(0, h) as pair:
                    for parity in range(2):
                        block_body(pair * 2 + first + parity, parity, pair + pairs, 2)
                block_body(h * 2 + first, 0, h + pairs, 1)
                block_body(h * 2 + first + 1, 1, h + pairs, 0)
                first, pairs = first + h * 2 + 2, pairs + h + 1

                for t in range(NT + 2):
                    if t < NT:
                        act.wait_ge(sem(f"y_in{t}"), 32 * (l + 1))
                        act.activation(y1[t], y1[t], ACT.Identity, scale=gate[:, 0, t:t + 1]).then_inc(sem("y_scaled"), 1)
                    if 1 <= t <= NT:
                        act.wait_ge(sem("x_moe"), at("x_moe", l, t))
                        norm1_square(l + 1, t - 1)
                    if t >= 2:
                        norm1_scale(l + 1, t - 2)
            act.wait_ge(sem("out_done"), 16 * 2 * DEPTH)

        @block.vector
        def _(dve):
            steps = [0]

            def link(ins):
                steps[0] += 1
                ins.then_inc(sem("dve_step"), 1)
                dve.wait_ge(sem("dve_step"), steps[0])

            def bc(ap, n):
                return ap.unsqueeze(len(ap.shape)).to_broadcast([*ap.shape, n])

            def mid(ap, n):
                return ap.unsqueeze(1).to_broadcast([P, n, *ap.shape[1:]])

            dve.wait_ge(sem("consts_loaded"), 48)
            dve.tensor_copy(upper[:, :], rt[:, 0:P]).then_inc(sem("upper_ready"), 1)
            dve.memset(ones[:, :], 1.0).then_inc(sem("upper_ready"), 1)
            dve.wait_ge(sem("upper_ready"), 2)

            def piece_add(l, g):
                dve.wait_ge(sem("ada_read"), at("ada_read", l, 2 * g + 2))
                if l == 0 and g < 4:
                    dve.wait_ge(sem("bias0_in"), 16)
                else:
                    dve.wait_ge(sem("bias_in"), 16 * (12 * l + g - 3))
                if 0 < g < 4:
                    dve.wait_ge(sem("modc_part"), at("modc_part", l, g))
                elif g == 4:
                    dve.wait_ge(sem("modc_psum"), at("modc_psum", l, 1))
                elif g > 4 or l:
                    dve.wait_ge(sem("piece_out"), at("piece_out", l, 16 * (g - 4)) if g else at("piece_out", l, 0))
                bias = bias0[:, g * N:(g + 1) * N] if l == 0 and g < 4 else bpiece
                dve.tensor_tensor(piece, ps[0:2, ada_bank(l, g), :], bias, ALU.add).then_inc(sem("piece_done"), 1)

            def modc_out(l):
                dve.wait_ge(sem("modc_psum"), at("modc_psum", l, 1))
                link(dve.tensor_copy(modc[:, :, :].rearrange("p k c -> p (k c)"), ps[:, 7, 0:32]))
                if l == 0:
                    dve.wait_ge(sem("norm1_loaded"), 16 * DEPTH)
                dve.scalar_tensor_tensor(out=modc[:, KD:, :], in0=modc[:, KD:, :], scalar=1.0,
                                         in1=bc(cols[:, KD * (1 + l):KD * (2 + l)], 2), op0=ALU.add, op1=ALU.mult
                                         ).then_inc(sem("a1_ready"), 1)

            def final_norm(t):
                dve.wait_ge(sem("rstd1"), at("rstd1", DEPTH, t + 1))
                dve.scalar_tensor_tensor(out=x[:, t, :], in0=x[:, t, :], scalar=stat[:, 8 + t:9 + t], in1=frow,
                                         op0=ALU.mult, op1=ALU.mult).then_inc(sem("y_final"), 1)

            for g in range(4):
                piece_add(0, g)
            modc_out(0)
            first = pairs = 0
            for l in range(DEPTH):
                def split_lo(i):
                    dve.wait_ge(sem("w_hi"), at("w_hi", l, i + 1))
                    dve.tensor_tensor(wL[:, i % HLS, :], raw[:, POS["w", l, i] % RAWS, :], f32(wH[:, i % HLS, :]),
                                      ALU.subtract).then_inc(sem("w_lo"), 1)

                split_lo(0)
                for k in range(KD):
                    dve.wait_ge(sem("h_hi"), at("h_hi", l, k + 1))
                    dve.tensor_tensor(actLk[:, k, :], hf[:, k % 2, :], f32(actHk[:, k, :]), ALU.subtract
                                      ).then_inc(sem("h_lo"), 1)
                    if k == 2:
                        split_lo(1)
                split_lo(2)
                dve.wait_ge(sem("params_loaded"), at("params_loaded", l, 15 * 16))
                link(dve.tensor_scalar(gains[:, 0, :], gains[:, 0, :], float(HD) ** -0.5, None, ALU.mult))
                for qk in range(2):
                    dve.tensor_tensor(tabs[:, :, qk, 0, :], tabs[:, :, qk, 0, :], mid(gains[:, qk, :], NT), ALU.mult
                                      ).then_inc(sem("tabs"), 1)
                    for half in range(2):
                        sn = tabs[:, :, qk, 1, :].rearrange("p t (x h f) -> p t x h f", x=2, h=2)[:, :, :, half, :]
                        gsw = gains[:, qk, :].rearrange("p (x h f) -> p x h f", x=2, h=2)[:, :, 1 - half, :]
                        dve.tensor_tensor(sn, sn, mid(gsw, NT), ALU.mult).then_inc(sem("tabs"), 1)
                def q_lo(t):
                    dve.wait_ge(sem("q_hi"), at("q_hi", l, t + 1))
                    dve.tensor_tensor(qhl[:, :, 1, :], mrg[:, ORDER[t], 0:512].rearrange("p (h d) -> p h d", h=NH),
                                      f32(qhl[:, :, 0, :]), ALU.subtract).then_inc(sem("q_lo"), 1)

                dve.wait_ge(sem("tabs"), at("tabs", l, 6))
                done = 3
                for gi in range(4 * NT):
                    nb, t = divmod(gi, NT)
                    if t == 0:
                        while done < min(8, 2 * nb + 4):
                            split_lo(done)
                            done += 1
                    if nb == 3 and t == 0:
                        kf = kv[:, :, 0:P].rearrange("p j (v d) -> p j v d", v=NKV)
                        for v in range(NKV):
                            dve.wait_ge(sem("k_hi"), at("k_hi", l, v + 1))
                            dve.tensor_tensor(kdup[1][:, :, v, :, :], kf[:, :, v, :].unsqueeze(2).to_broadcast([P, NKEY, 2, HD]),
                                              f32(kdup[0][:, :, v, :, :]), ALU.subtract).then_inc(sem("k_lo"), 1)
                        q_lo(0)
                    if nb < 2:
                        H = NH if nb == 0 else NKV
                        final = "q_final" if nb == 0 else "k_final"
                        j = t if t < CTX else CTXK
                        W = H * HD
                        src = mrg[:, t, 0:512] if nb == 0 else kv[:, j, 0:P]
                        heads = lambda ap: ap.rearrange("p (h d) -> p h d", d=HD)
                        half = lambda ap, i: ap.rearrange("p (x h f) -> p x h f", h=2, f=16)[:, :, i, :]
                        t1, t2 = pbuf[:, 512:512 + W], pbuf[:, 1024:1024 + W]
                        for i in ([gi] if t == 0 else []) + ([gi + 1] if t + 1 < NT else []):
                            dve.wait_ge(sem("sq"), at("sq", l, i + 1))
                            sq0 = 512 if nb == 0 else 768
                            dve.reduce_sum(stat[:, 16 + 8 * (i % 2):16 + 8 * (i % 2) + H], heads(mrg[:, i % NT, sq0:sq0 + W]), X
                                           ).then_inc(sem("ssqk"), 1)
                        dve.wait_ge(sem("rqk"), at("rqk", l, gi + 1))
                        dve.wait_ge(sem("proj_read"), at("proj_read", l, gi + 1))
                        if nb == 1:
                            dve.wait_ge(sem("kv_raw"), at("kv_raw", l, t + 1))
                        link(dve.tensor_tensor(heads(src), heads(src), bc(stat[:, 32 + 8 * (gi % 2):32 + 8 * (gi % 2) + H], HD), ALU.mult))
                        link(dve.tensor_tensor(heads(t1), heads(src), mid(tabs[:, t, nb, 0, :], H), ALU.mult))
                        for i in range(2):
                            sn = tabs[:, t, nb, 1, :].rearrange("p (x h f) -> p x h f", x=2, h=2)[:, :, i, :]
                            o4 = t2.rearrange("p (n x h f) -> p n x h f", x=2, h=2, f=16)[:, :, :, i, :]
                            i4 = src.rearrange("p (n x h f) -> p n x h f", x=2, h=2, f=16)[:, :, :, 1 - i, :]
                            link(dve.tensor_tensor(o4, i4, mid(sn, H), ALU.mult))
                        dve.tensor_tensor(src, t1, t2, ALU.add).then_inc(sem(final), 1)
                        dve.wait_ge(sem(final), at(final, l, t + 1))
                    elif nb == 3:
                        dve.wait_ge(sem("proj_read"), at("proj_read", l, gi + 1))
                        dve.tensor_tensor(z[:, t, :], z[:, t, :], ps[:, gi % 8, 256:512], ALU.mult
                                          ).then_inc(sem("z_done"), 1)
                for v in range(NKV):
                    dve.wait_ge(sem("v_hi"), at("v_hi", l, v + 1))
                    dve.tensor_tensor(vv[v][:, :, HD:], kv[:, :, P + HD * v:P + HD * (v + 1)], f32(vv[v][:, :, 0:HD]),
                                      ALU.subtract).then_inc(sem("v_lo"), 1)

                def sgu_out(g):
                    dve.wait_ge(sem("sgu_psum"), at("sgu_psum", l, g + 1))
                    u_ = mrg[:, :, 512 + 64 * g:576 + 64 * g]
                    dve.scalar_tensor_tensor(out=u_, in0=ps[:, g, 0:320].rearrange("p (t c) -> p t c", t=NT),
                                             scalar=sgb[:, g:g + 1], in1=u_, op0=ALU.add, op1=ALU.mult
                                             ).then_inc(sem("sgu_done"), 1)

                for g in range(4):
                    sgu_out(g)

                def o_high(g):
                    t, r = divmod(g, 2)
                    dst = mrg[:, ORDER[t], 256 * r:256 * r + 256].rearrange("p (h d) -> p h d", h=4)
                    dve.wait_ge(sem("o_low"), at("o_low", l, g + 1))
                    c = (8 * t + 4 * r) % 16
                    link(dve.reciprocal(rinv[:, 4 * r:4 * r + 4], rsum[:, c:c + 4]))
                    dve.tensor_tensor(dst, ps[:, 6, :].rearrange("p (h s d) -> p h s d", h=4, s=2)[:, :, 0, :], dst,
                                      ALU.add).then_inc(sem("o_read"), 1)
                    dve.wait_ge(sem("o_read"), at("o_read", l, g + 1))
                    dve.tensor_tensor(dst, dst, bc(rinv[:, 4 * r:4 * r + 4], HD), ALU.mult).then_inc(sem("attn_done"), 1)

                def normalise(t):
                    dve.wait_ge(sem("rstd3"), at("rstd3", l, t + 1))
                    dve.wait_ge(sem("attn_done"), at("attn_done", l, 2 * t + 2))
                    for j, (a, b) in enumerate(((0, 512), (512, 768), (768, 1024))):
                        c = 48 + 3 * t + j
                        dve.tensor_scalar(mrg[:, ORDER[t], a:b], mrg[:, ORDER[t], a:b], stat[:, c:c + 1], None, ALU.mult
                                          ).then_inc(sem("mrg_ready"), 1)

                q_lo(1)
                for u in range(NT * NH + 1):
                    if u < NT * NH:
                        t, h = divmod(u, NH)
                        keys = 5 * P if t else P
                        dve.wait_ge(sem("scores"), at("scores", l, u + 1))
                        if u >= 2:
                            dve.wait_ge(sem("prob"), at("prob", l, u - 1))
                        dve.tensor_reduce(nmax[:, u % 2:u % 2 + 1], flat[:, 2 * N * (u % 2):2 * N * (u % 2) + keys], X, ALU.max, negate=True).then_inc(sem("nmax"), 1)
                    if u >= 1:
                        v = u - 1
                        keys = 5 * P if v >= NH else P
                        dve.wait_ge(sem("pT_hi"), at("pT_hi", l, v + 1))
                        dve.tensor_tensor(pTL[:, v % 2, 0:keys], flat[:, 4 * N:4 * N + keys],
                                          f32(pTH[:, v % 2, 0:keys]), ALU.subtract).then_inc(sem("pT_lo"), 1)
                    if u >= 2 and (u - 2) % 4 == 3:
                        o_high((u - 2) // 4)
                    if u in W_AT:
                        split_lo(W_AT[u])
                    if u >= 13 and u % 8 == 5:
                        normalise(u // 8 - 1)
                    if u < NLT * NH:
                        t, h = divmod(u, NH)
                        if h == 2 and t + 2 < NT:
                            q_lo(t + 2)
                    if u in PIECE_AT:
                        piece_add(l, 4 + PIECE_AT.index(u))
                o_high(2 * NT - 1)
                normalise(NT - 1)
                for k in range(KD):
                    dve.wait_ge(sem("mT_hi"), at("mT_hi", l, 2 * k + 2))
                    on = cols[:, k:k + 1]
                    dve.scalar_tensor_tensor(out=actLk[:, k, 0:512], in0=ps[:, 5 + 2 * (k % 2), :], scalar=on, in1=f32(actHk[:, k, 0:512]),
                                             op0=ALU.mult, op1=ALU.subtract).then_inc(sem("mT_lo"), 1)
                    dve.scalar_tensor_tensor(out=actLk[:, k, 512:640], in0=ps[:, 6, 0:P], scalar=on,
                                             in1=f32(actHk[:, k, 512:640]), op0=ALU.mult, op1=ALU.subtract
                                             ).then_inc(sem("mT_lo"), 1)
                    if k == 1:
                        split_lo(9)
                for i in range(10, 12):
                    split_lo(i)
                dve.wait_ge(sem("scale2_row"), at("scale2_row", l, 32))
                dve.wait_ge(sem("norm2_row"), at("norm2_row", l, 16))
                for c in range(2):
                    dve.scalar_tensor_tensor(out=arow[:, c, :], in0=arow[:, c, :], scalar=1.0, in1=n2row,
                                             op0=ALU.add, op1=ALU.mult).then_inc(sem("a2_row"), 1)
                dve.wait_ge(sem("gate1_row"), at("gate1_row", l, 32))
                dve.wait_ge(sem("mT_psum"), at("mT_psum", l, KD))
                for i in range(2 * NT):
                    nb, t = divmod(i, NT)
                    dve.wait_ge(sem("oproj_psum"), at("oproj_psum", l, i + 1))
                    if i >= 4:
                        dve.wait_ge(sem("x_attn"), at("x_attn", l, i - 3))
                    dve.tensor_tensor(otmp[:, i % 4, :], ps[:, i % 8, :], grow[:, int(t == CTX), nb * N:(nb + 1) * N],
                                      ALU.mult).then_inc(sem("oproj"), 1)
                dve.wait_ge(sem("a2_row"), at("a2_row", l, 2))
                dve.wait_ge(sem("shift2_row"), at("shift2_row", l, 32))
                for t in range(NT):
                    c = int(t == CTX)
                    dve.wait_ge(sem("rstd2"), at("rstd2", l, t + 1))
                    dve.wait_ge(sem("x_attn"), at("x_attn", l, NT + t + 1))
                    if t >= 2:
                        dve.wait_ge(sem(f"h2_stored{t % 2}"), at(f"h2_stored{t % 2}", l, 16 * (t // 2)))
                        dve.wait_ge(sem("h2T_psum"), at("h2T_psum", l, t - 1))
                    hb = h2b[:, t % 2, :]
                    link(dve.scalar_tensor_tensor(out=hb, in0=x[:, t, :], scalar=stat[:, 8 + t:9 + t], in1=arow[:, c, :],
                                                  op0=ALU.mult, op1=ALU.mult))
                    dve.tensor_tensor(hb, hb, srow[:, c, :], ALU.add).then_inc(sem("h2"), 1)
                    if l + 1 < DEPTH and t in (0, NT - 1):
                        piece_add(l + 1, t // (NT - 1))
                dve.wait_ge(sem("ss2"), at("ss2", l, NT))

                dve.wait_ge(sem("logits"), at("logits", l, NT))
                pri, thr, bidx = pcon[:, 0:4], pcon[:, 4:9], pcon[:, 9:9 + LB]
                tidx, toff = pcon[:, 40:41], pcon[:, 41:46]
                link(dve.tensor_tensor(lg, ps[:, 4, 0:100].rearrange("p (t n) -> p t n", t=NT), mid(rb[:, :], NT), ALU.add))
                gl, el = lg[:, :, 0:NG], lg[:, :, NG:]

                def first_max(v, m, out):
                    link(dve.tensor_reduce(m, v, X, ALU.max))
                    link(dve.tensor_tensor(eq, v, bc(m, 4), ALU.is_equal))
                    link(dve.tensor_tensor(eq, eq, mid(pri, NT), ALU.mult))
                    link(dve.tensor_reduce(sm, eq, X, ALU.max))
                    link(dve.tensor_tensor(out, eq, bc(sm, 4), ALU.is_equal))

                first_max(gl, gm, og)
                dve.tensor_tensor(ex, gl, bc(gm, 4), ALU.subtract).then_inc(sem("rt_exp_in"), 1)
                link(dve.tensor_tensor(pr, el.rearrange("p t (g e) -> p t g e", g=4), bc(og, 4), ALU.mult))
                link(dve.reduce_sum(es, pr.rearrange("p t g e -> p t e g"), X))
                first_max(es, em1, o1)
                link(dve.scalar_tensor_tensor(out=e2, in0=o1, scalar=-1e30, in1=es, op0=ALU.mult, op1=ALU.add))
                first_max(e2, em2, o2)
                dve.wait_ge(sem("rt_exp"), at("rt_exp", l, 1))
                link(dve.reduce_sum(pg, ex, X))
                link(dve.reciprocal(pg, pg))
                dve.tensor_tensor(d_, em2, em1, ALU.subtract).then_inc(sem("rt_exp_in"), 1)
                for c, o in enumerate((o1, o2)):
                    link(dve.tensor_tensor(M[:, c].rearrange("p t (g e) -> p t g e", g=4), bc(og, 4),
                                           o.unsqueeze(2).to_broadcast([P, NT, 4, 4]), ALU.mult))
                dve.tensor_tensor(Mb, M[:, 0], M[:, 1], ALU.add).then_inc(sem("choice"), 1)
                if l + 1 < DEPTH:
                    piece_add(l + 1, 2)
                def m_split(i, b):
                    dve.wait_ge(sem(f"m_hi{i}"), b + 1)
                    dve.tensor_tensor(wL[:, i, :], raw[:, i, :], f32(wH[:, i, :]), ALU.subtract).then_inc(sem(f"m_lo{i}"), 1)

                dve.wait_ge(sem("counts_psum"), at("counts_psum", l, 1))
                link(dve.tensor_copy(pos, ps[:, 5, 0:NT * 16]))
                link(dve.tensor_copy(cnt, ps[:, 4, 0:16]))
                link(dve.tensor_tensor(cmp5, bc(cnt, 5), mid(thr, 16), ALU.is_gt))
                link(dve.reduce_sum(nb_, cmp5, X))
                link(dve.tensor_tensor_scan(incl, pcon[:, 46:62], nb_, 0.0, ALU.mult, ALU.add))
                link(dve.tensor_tensor(base, incl, nb_, ALU.subtract))
                Mf = M.rearrange("p c t e -> p c (t e)")
                link(dve.tensor_tensor(pr2.rearrange("p (c n) -> p c n", c=2), Mf, mid(pos, 2), ALU.mult))
                link(dve.reduce_sum(q, pr2.rearrange("p (c e) -> p c e", e=16), X))
                M10 = M.rearrange("p c t e -> p (c t) e")
                link(dve.tensor_tensor(pr2.rearrange("p (c e) -> p c e", e=16), M10, mid(base, 10), ALU.mult))
                link(dve.reduce_sum(eb, pr2.rearrange("p (c e) -> p c e", e=16), X))
                link(dve.tensor_tensor(pr2[:, 0:40].rearrange("p (c e) -> p c e", e=4), bc(q, 4), mid(thr[:, 1:5], 10), ALU.is_ge))
                link(dve.reduce_sum(qd, pr2[:, 0:40].rearrange("p (c e) -> p c e", e=4), X))
                link(dve.tensor_tensor(eb, eb, qd, ALU.add))
                link(dve.scalar_tensor_tensor(out=q, in0=qd, scalar=-128.0, in1=q, op0=ALU.mult, op1=ALU.add))
                link(dve.scalar_tensor_tensor(out=qd, in0=eb, scalar=128.0, in1=q, op0=ALU.mult, op1=ALU.add))
                link(dve.tensor_copy(slot[:, :], qd))
                link(dve.tensor_tensor(one_r, bc(q, P), mid(iota[:, :], 10), ALU.is_equal))
                link(dve.tensor_tensor(oneb, bc(eb, LB), mid(bidx, 10), ALU.is_equal))
                link(dve.tensor_scalar(tl[:, :, 0, :], oneb, tidx, None, ALU.mult))
                for c in range(2):
                    link(dve.tensor_tensor(tl[:, c * NT:(c + 1) * NT, 1, :], oneb[:, c * NT:(c + 1) * NT, :], bc(toff, LB), ALU.mult))
                dve.sem_inc(sem("lists"), 1)
                for i in range(3):
                    n = min(10, LB - 10 * i)
                    cbv = pr2[:, 0:16 * n].rearrange("p (b e) -> p b e", e=16)
                    link(dve.tensor_tensor(cbv, mid(incl, n), bc(bidx[:, 10 * i:10 * i + n], 16), ALU.is_le))
                    link(dve.reduce_sum(eb26[:, 1 + 10 * i:1 + 10 * i + n], cbv, X))
                link(dve.tensor_scalar(eb26[:, 1:1 + LB], eb26[:, 1:1 + LB], float(NE - 1), None, ALU.min))
                evens = bidx.rearrange("p (b two) -> p b two", two=2)[:, 2:, 0]
                link(dve.tensor_tensor(pr2[:, 0:LB // 2 - 2], incl[:, 15:16].to_broadcast([P, LB // 2 - 2]), evens, ALU.is_gt))
                link(dve.reduce_sum(eb26[:, 0:1], pr2[:, 0:LB // 2 - 2], X))
                link(dve.tensor_copy(ctl[0:1, 0:1 + LB], eb26[0:1, 0:1 + LB]))
                dve.wait_ge(sem("list_psum"), at("list_psum", l, 1))
                idf, empt = pr2[:, 0:2 * LB].rearrange("p (s b) -> p s b", s=2), pr2[:, 2 * LB:3 * LB]
                link(dve.tensor_copy(idf.rearrange("p s b -> p (s b)"), ps[:, 0, 0:2 * LB]))
                link(dve.tensor_scalar(empt, idf[:, 0, :], 0.0, float(NOROW), ALU.is_equal, ALU.mult))
                link(dve.scalar_tensor_tensor(out=idf[:, 0, :], in0=idf[:, 0, :], scalar=-1.0, in1=idf[:, 1, :],
                                              op0=ALU.add, op1=ALU.add))
                link(dve.tensor_tensor(idf[:, 0, :], idf[:, 0, :], empt, ALU.add))
                link(dve.tensor_scalar(idf[:, 0, :], idf[:, 0, :], 0.0, None, ALU.max))
                link(dve.tensor_copy(idxs[:, :], idf[:, 0, :]))
                dve.sem_inc(sem("ctl_ready"), 1)
                m_split(0, first)
                if l + 1 < DEPTH:
                    piece_add(l + 1, 3)
                m_split(1, first)
                if l + 1 < DEPTH:
                    modc_out(l + 1)
                dve.wait_ge(sem("rt_exp"), at("rt_exp", l, 2))
                link(dve.tensor_scalar(em1, d_, 1.0, None, ALU.add))
                link(dve.reciprocal(em1, em1))
                link(dve.tensor_tensor(gate[:, 0, :], em1, pg, ALU.mult))
                link(dve.tensor_tensor(gate[:, 1, :], gate[:, 0, :], d_, ALU.mult))

                def x_lo(h, b):
                    dve.wait_ge(sem("m_xh"), b * 2 + h + 1)
                    dve.tensor_tensor(actL[:, N * h:N * h + N], ps[:, 1 + h, :], f32(actH[:, N * h:N * h + N]),
                                      ALU.subtract).then_inc(sem("m_xl"), 1)

                def block_body(b, parity, pair, left):
                    if left >= 1:
                        x_lo(0, b + 1)
                    dve.wait_ge(sem("m_sg"), b + 1)
                    dve.tensor_tensor(hid[:, F:2 * F], hid[:, 0:F], ps[:, 0, F:2 * F], ALU.mult).then_inc(sem("m_hid"), 1)
                    m_split(2, b)
                    dve.wait_ge(sem("m_hh"), b + 1)
                    dve.tensor_tensor(hTL.rearrange("p k n -> p (k n)"), ps[:, 3, 0:F], f32(hTH.rearrange("p k n -> p (k n)")),
                                      ALU.subtract).then_inc(sem("m_hl"), 1)
                    if left >= 1:
                        m_split(1, b + 1)
                        x_lo(1, b + 1)
                    if left >= 2:
                        m_split(0, b + 2)
                    dve.wait_ge(sem("m_w2"), b + 1)
                    dve.wait_ge(sem(f"m_ys{parity}"), pair * 16 + 16)
                    dve.tensor_copy(yo[parity][:, N:], ps[:, 5, :]).then_inc(sem("m_yd"), 1)

                h = dve.value_load(ctl[0:1, 0:1], min_val=MINB // 2 - 2, max_val=MAXB // 2 - 2) + 1
                if l == 0:
                    dve.sem_inc(sem("m_yd"), 1)
                    dve.sem_inc(sem("m_ys1"), 16)
                x_lo(0, first)
                x_lo(1, first)
                m_split(0, first + 1)
                with dve.Fori(0, h) as pair:
                    for parity in range(2):
                        block_body(pair * 2 + first + parity, parity, pair + pairs, 2)
                block_body(h * 2 + first, 0, h + pairs, 1)
                block_body(h * 2 + first + 1, 1, h + pairs, 0)
                first, pairs = first + h * 2 + 2, pairs + h + 1
                dve.sem_inc(sem("moe_split_done"), 1)
                dve.wait_ge(sem("gate2_row"), at("gate2_row", l, 32))
                for t in range(NT):
                    c = int(t == CTX)
                    dve.wait_ge(sem(f"y_in{t}"), 32 * (l + 1))
                    dve.wait_ge(sem("y_scaled"), at("y_scaled", l, t + 1))
                    link(dve.scalar_tensor_tensor(out=y1[t], in0=y2[t], scalar=gate[:, 1, t:t + 1], in1=y1[t], op0=ALU.mult, op1=ALU.add))
                    link(dve.tensor_tensor(y1[t], y1[t], grow[:, c, :], ALU.mult))
                    dve.tensor_tensor(x[:, t, :], x[:, t, :], y1[t], ALU.add).then_inc(sem("x_moe"), 1)
                    if l == DEPTH - 1 and t == 0:
                        dve.wait_ge(sem("final_row"), 16)
                    if l == DEPTH - 1 and t:
                        final_norm(t - 1)
            dve.wait_ge(sem("x_moe"), at("x_moe", DEPTH - 1, NT))
            final_norm(NT - 1)

        @block.tensor
        def _(pe):
            pe.wait_ge(sem("c_silu"), 1)
            pe.wait_ge(sem("ident_loaded"), 16)

            def three(out, aH, aL, slot_, cols_, first, last):
                pe.matmul(out, aH, wH[:, slot_, cols_], start=first, stop=False)
                pe.matmul(out, aH, wL[:, slot_, cols_], start=False, stop=False)
                return pe.matmul(out, aL, wH[:, slot_, cols_], start=False, stop=last)

            def ada_mm(l, j):
                g, kt = divmod(j, KD)
                if kt == 0 and (g >= 2 or l):
                    pe.wait_ge(sem("piece_done"), at("piece_done", l, g - 1 if l == 0 and g < 4 else g))
                if kt % 4 == 0:
                    unit_loaded(pe, "ada", l, j // 4)
                w = raw[:, POS["ada", l, j // 4] % RAWS, :].rearrange("p (k n) -> p k n", k=4)
                m = pe.matmul(ps[0:2, ada_bank(l, g), :], csil[:, kt, :], w[:, kt % 4, :], start=(kt == 0), stop=(kt == KD - 1))
                if kt % 4 == 3:
                    m.then_inc(sem("ada_read"), 1)

            def modc_cols(l, g):
                pe.wait_ge(sem("piece_done"), at("piece_done", l, g + 1))
                for j in range(4):
                    m = pe.transpose(ps[:, 7, 8 * g + 2 * j:8 * g + 2 * j + 2], piece[:, j * P:(j + 1) * P], ident[0:2, 0:2])
                m.then_inc(sem("modc_psum" if g == 3 else "modc_part"), 1)

            def ada_piece(l, g):
                for j in range(KD * g, KD * (g + 1)):
                    ada_mm(l, j)

            for g in range(5):
                if g < 4:
                    ada_piece(0, g)
                if g:
                    modc_cols(0, g - 1)
            first = pairs = 0
            for l in range(DEPTH):
                pe.wait_ge(sem("xr_ready"), at("xr_ready", l, NT))

                def h_chunk(k):
                    if k >= 1:
                        pe.wait_ge(sem("h_full"), at("h_full", l, 2 * k))
                    for t in range(NT):
                        bank = 6 if t == CTX else 5 + 2 * (k % 2)
                        m = pe.transpose(ps[:, bank, P * (t % 4):P * (t % 4) + P], xr[t][:, k * P:(k + 1) * P], ident[:, :])
                    m.then_inc(sem("hT_psum"), 1)

                def keys_T(j):
                    if j >= 2:
                        pe.wait_ge(sem("kk"), at("kk", l, j - 1))
                    for v in range(NKV):
                        for part in range(2):
                            c = 2 * v + part
                            m = pe.transpose(ps[:, 4 + j % 2, c * P:(c + 1) * P],
                                             f32(kdup[part][:, j, v, :, :].rearrange("p s d -> p (s d)")), ident[:, :])
                    m.then_inc(sem("kT_psum"), 1)

                h_chunk(0)
                h_chunk(1)
                for i in range(8):
                    nb, half = divmod(i, 2)
                    for k in range(4):
                        kt = 4 * half + k
                        if nb == 0:
                            pe.wait_ge(sem("h_lo"), at("h_lo", l, kt + 1))
                        if k == 0:
                            pe.wait_ge(sem("w_lo"), at("w_lo", l, i + 1))
                        for t in range(NT):
                            gi = nb * NT + t
                            if kt == 0 and gi >= 8:
                                pe.wait_ge(sem("proj_read"), at("proj_read", l, gi - 7))
                            m = three(ps[:, gi % 8, :], actHk[:, kt, t * P:(t + 1) * P], actLk[:, kt, t * P:(t + 1) * P],
                                      i % HLS, slice(k * N, (k + 1) * N), kt == 0, kt == KD - 1)
                            if kt == KD - 1:
                                m.then_inc(sem("proj"), 1)
                        if k == 3 and half == 0:
                            m.then_inc(sem("w_used"), 1)
                        if nb == 0 and kt + 2 < KD:
                            h_chunk(kt + 2)
                        if nb == 3 and kt == 4:
                            m.then_inc(sem("front_used"), 1)
                            pe.wait_ge(sem("proj_read"), at("proj_read", l, 15))
                            pe.wait_ge(sem("taps_loaded"), at("taps_loaded", l, 32))
                            for g in range(4):
                                m = pe.transpose(ps[:, 6, g * P:(g + 1) * P], sgw[:, g, :], ident[:, :])
                            m.then_inc(sem("sgT_psum"), 1)
                        if nb == 3 and kt in (5, 6):
                            pe.wait_ge(sem("k_lo"), at("k_lo", l, NKV))
                            keys_T(kt - 5)
                pe.wait_ge(sem("z_done"), at("z_done", l, NT))
                for j in range(2, NKEY):
                    pe.matmul(ps[:, j - 2, 0:320], sgT[:, j - 2, :], sv[:, :, 64 * (j - 2):64 * (j - 2) + 64], start=True, stop=True
                              ).then_inc(sem("sgu_psum"), 1)
                    keys_T(j)

                def q_round(t, r):
                    if r == 0:
                        pe.wait_ge(sem("q_lo"), at("q_lo", l, t + 1))
                    if t or r:
                        pe.wait_ge(sem("qT"), at("qT", l, 2 * t + r))
                    for h in range(4):
                        m = pe.transpose(ps[:, 7, h * P:(h + 1) * P],
                                         f32(qhl[:, 4 * r + h, :, :].rearrange("p s d -> p (s d)")), ident[:, :])
                    m.then_inc(sem("qT_psum"), 1)

                q_round(0, 0)
                q_round(0, 1)
                pe.wait_ge(sem("kk"), at("kk", l, NKEY))
                pe.wait_ge(sem("v_lo"), at("v_lo", l, NKV))
                pe.wait_ge(sem("sgu_done"), at("sgu_done", l, 4))
                for u in range(NT * NH + 2):
                    if u < NT * NH:
                        t, h = divmod(u, NH)
                        v = h // 4
                        if h == 0:
                            pe.wait_ge(sem("qT"), at("qT", l, 2 * t + 2))
                        if u >= 2:
                            pe.wait_ge(sem("prob"), at("prob", l, u - 1))
                        b0 = 2 * (u % 2)
                        spans = [(0, 0, 512), (1, 512, 640)] if t else [(0, 640, 768)]
                        for bk, a, b in spans:
                            pe.matmul(ps[:, b0 + bk, 0:b - a], qT[:, t % 2, h, :], kk[:, 2 * v, a:b], start=True, stop=False)
                            m = pe.matmul(ps[:, b0 + bk, 0:b - a], qT[:, t % 2, h, :], kk[:, 2 * v + 1, a:b], start=False, stop=True)
                        m.then_inc(sem("scores"), 1)
                    if 1 <= u <= NT * NH:
                        w = u - 1
                        nk = 5 if w >= NH else 1
                        pe.wait_ge(sem("prob"), at("prob", l, w + 1))
                        if w:
                            pe.wait_ge(sem("pT_lo"), at("pT_lo", l, w))
                        for c in range(nk):
                            m = pe.transpose(ps[:, 4 + c // 4, (c % 4) * P:(c % 4) * P + P], prob[:, w % 2, c * P:(c + 1) * P], ident[:, :])
                        m.then_inc(sem("pT_psum"), 1)
                    if u >= 2:
                        w = u - 2
                        t, h = divmod(w, NH)
                        pe.wait_ge(sem("pT_lo"), at("pT_lo", l, w + 1))
                        if w % 4 == 0 and w:
                            pe.wait_ge(sem("o_read"), at("o_read", l, w // 4))
                        slots = range(5) if t else [CTXK]
                        o = (h % 4) * P
                        for c, j in enumerate(slots):
                            pe.matmul(ps[:, 6, o:o + P], pTH[:, w % 2, c * P:(c + 1) * P], vv[h // 4][:, j, :],
                                      start=(c == 0), stop=False, skip_group_check=True)
                            m = pe.matmul(ps[:, 6, o:o + HD], pTL[:, w % 2, c * P:(c + 1) * P], vv[h // 4][:, j, 0:HD],
                                          start=False, stop=(c == len(slots) - 1), skip_group_check=True)
                        m.then_inc(sem("pv"), 1)
                    if u < NLT * NH:
                        t, h = divmod(u, NH)
                        if h < 2:
                            if h == 0 and t:
                                pe.wait_ge(sem("piece_done"), at("piece_done", l, 4 + sum(p_ < u for p_ in PIECE_AT)))
                            q_round(t + 1, h)
                        elif h == 2:
                            pe.wait_ge(sem("qT"), at("qT", l, 2 * t + 4))
                    if u < NT * NH:
                        for j in range(sum(ADA_AT[:u]), sum(ADA_AT[:u + 1])):
                            ada_mm(l, 4 * KD + j)
                pe.wait_ge(sem("o_read"), at("o_read", l, 2 * NT))

                def merged_chunk(k):
                    for t in range(NT):
                        if k == 0:
                            pe.wait_ge(sem("mrg_ready"), at("mrg_ready", l, 3 * ORDER.index(t) + 3))
                        if t == 0 and k >= 2:
                            pe.wait_ge(sem("mT_lo"), at("mT_lo", l, 2 * k - 2))
                        if t == CTX and k >= 1:
                            pe.wait_ge(sem("mT_lo"), at("mT_lo", l, 2 * k))
                        bank = 6 if t == CTX else 5 + 2 * (k % 2)
                        m = pe.transpose(ps[:, bank, P * (t % 4):P * (t % 4) + P], mrg[:, t, k * P:(k + 1) * P], ident[:, :])
                    m.then_inc(sem("mT_psum"), 1)

                merged_chunk(0)
                merged_chunk(1)
                for i in range(8, 12):
                    nb, half = divmod(i - 8, 2)
                    for k in range(4):
                        kt = 4 * half + k
                        if nb == 0:
                            pe.wait_ge(sem("mT_lo"), at("mT_lo", l, 2 * kt + 2))
                        if k == 0:
                            pe.wait_ge(sem("w_lo"), at("w_lo", l, i + 1))
                        for t in range(NT):
                            gi = nb * NT + t
                            if kt == 0 and gi >= 8:
                                pe.wait_ge(sem("oproj"), at("oproj", l, gi - 7))
                            m = three(ps[:, gi % 8, :], actHk[:, kt, t * P:(t + 1) * P], actLk[:, kt, t * P:(t + 1) * P],
                                      i % HLS, slice(k * N, (k + 1) * N), kt == 0, kt == KD - 1)
                            if kt == KD - 1:
                                m.then_inc(sem("oproj_psum"), 1)
                        if k == 3 and half == 0:
                            m.then_inc(sem("w_used"), 1)
                        if nb == 0 and kt + 2 < KD:
                            merged_chunk(kt + 2)
                if l + 1 < DEPTH:
                    pe.wait_ge(sem("oproj"), at("oproj", l, 7))
                    ada_piece(l + 1, 0)
                pe.wait_ge(sem("oproj"), at("oproj", l, 2 * NT))

                def h2_chunks(t):
                    pe.wait_ge(sem("h2"), at("h2", l, t + 1))
                    if t >= 2:
                        pe.wait_ge(sem("h2T"), at("h2T", l, t - 1))
                    for k in range(KD):
                        m = pe.transpose(ps[:, 2 * (t % 2) + k // 4, (k % 4) * P:(k % 4) * P + P], h2b[:, t % 2, k * P:(k + 1) * P], ident[:, :])
                    m.then_inc(sem("h2T_psum"), 1)
                    if l + 1 < DEPTH and t:
                        if t == 1:
                            modc_cols(l + 1, 0)
                        ada_mm(l + 1, 6 + 2 * t)
                        ada_mm(l + 1, 7 + 2 * t)

                h2_chunks(0)
                for t in range(NT):
                    if t + 1 < NT:
                        h2_chunks(t + 1)
                    pe.wait_ge(sem("h2T"), at("h2T", l, t + 1))
                    for k in range(KD):
                        m = pe.matmul(ps[:, 4, 20 * t:20 * t + 20], h2T[t % 2][:, k, :], rw[:, k, :], start=(k == 0), stop=(k == KD - 1))
                    m.then_inc(sem("logits"), 1)
                if l + 1 < DEPTH:
                    modc_cols(l + 1, 1)
                    ada_piece(l + 1, 2)
                pe.wait_ge(sem("choice"), at("choice", l, 1))
                pe.matmul(ps[:, 5, 0:NT * 16], upper[:, :], Mb, start=True, stop=False, skip_group_check=True)
                for t in range(NT - 1):
                    pe.matmul(ps[:, 5, (t + 1) * 16:NT * 16], ones[:, :], Mb[:, t, :].unsqueeze(1).to_broadcast([P, NT - 1 - t, 16]),
                              start=False, stop=(t == NT - 2), skip_group_check=True)
                for t in range(NT):
                    m = pe.matmul(ps[:, 4, 0:16], ones[:, :], Mb[:, t, :], start=(t == 0), stop=(t == NT - 1))
                m.then_inc(sem("counts_psum"), 1)
                pe.wait_ge(sem("lists"), at("lists", l, 1))
                for c in range(10):
                    m = pe.matmul(ps[:, 0, 0:2 * LB], one_r[:, c, :], tl[:, c, :, :].rearrange("p s b -> p (s b)"), start=(c == 0), stop=(c == 9))
                m.then_inc(sem("list_psum"), 1)
                if l + 1 < DEPTH:
                    modc_cols(l + 1, 2)
                    ada_piece(l + 1, 3)
                    modc_cols(l + 1, 3)

                def x_chunks(h, b, parity, pair):
                    if h == 0:
                        pe.wait_ge(sem(f"m_g{parity}"), (pair + 1) * 16)
                    for k in range(4):
                        m = pe.transpose(ps[:, 1 + h, k * P:(k + 1) * P], xg[:, parity, h * N + k * P:h * N + (k + 1) * P], ident[:, :])
                    m.then_inc(sem("m_tx"), 1)

                def w13(h, b):
                    pe.wait_ge(sem("m_xl"), b * 2 + h + 1)
                    pe.wait_ge(sem(f"m_lo{h}"), b + 1)
                    for k in range(4):
                        kt = 4 * h + k
                        m = three(ps[:, 0, :], xTH[:, kt, :], xTL[:, kt, :], h, slice(k * N, (k + 1) * N), kt == 0, kt == KD - 1)
                    m.then_inc(sem("m_w13"), 1)

                def block_body(b, parity, pair, left):
                    if left >= 1:
                        x_chunks(0, b + 1, 1 - parity, pair + parity)
                    w13(1, b)
                    if left >= 1:
                        x_chunks(1, b + 1, 1 - parity, pair + parity)
                    pe.wait_ge(sem("m_hid"), b + 1)
                    for k in range(2):
                        m = pe.transpose(ps[:, 3, k * P:(k + 1) * P], hid[:, F + k * P:F + (k + 1) * P], ident[:, :])
                    m.then_inc(sem("m_th"), 1)
                    if left >= 1:
                        w13(0, b + 1)
                    pe.wait_ge(sem("m_ya"), b + 1)
                    pe.wait_ge(sem("m_yd"), b + 1)
                    pe.wait_ge(sem("m_lo2"), b + 1)
                    pe.wait_ge(sem("m_hl"), b + 1)
                    for nb in range(2):
                        for k in range(2):
                            m = three(ps[:, 4 + nb, :], hTH[:, k, :], hTL[:, k, :], 2, slice(k * D + nb * N, k * D + nb * N + N),
                                      k == 0, k == 1)
                    m.then_inc(sem("m_w2"), 1)

                pe.wait_ge(sem("ctl_ready"), at("ctl_ready", l, 1))
                h = pe.value_load(ctl[0:1, 0:1], min_val=MINB // 2 - 2, max_val=MAXB // 2 - 2) + 1
                x_chunks(0, first, 0, pairs)
                x_chunks(1, first, 0, pairs)
                w13(0, first)
                with pe.Fori(0, h) as pair:
                    for parity in range(2):
                        block_body(pair * 2 + first + parity, parity, pair + pairs, 2)
                block_body(h * 2 + first, 0, h + pairs, 1)
                block_body(h * 2 + first + 1, 1, h + pairs, 0)
                first, pairs = first + h * 2 + 2, pairs + h + 1


def shape_constants():
    import numpy as np

    half = 16
    inv = (1.0 / (np.float32(10000.0) ** (np.arange(half, dtype=np.float32) * 2.0 / 32))).astype(np.float32)
    n = np.arange(NLT * P)
    ang = np.stack([(n // 64).astype(np.float32)[:, None] * inv, (n % 64).astype(np.float32)[:, None] * inv], 1)
    cos, sin = np.cos(ang), np.sin(ang)
    tab = np.zeros((P, NT, 2, 64), np.float32)
    tab[:, CTX, 0, :] = 1.0
    c = np.concatenate([cos, cos], -1).reshape(NLT, P, 64)
    s = np.concatenate([-sin, sin], -1).reshape(NLT, P, 64)
    tab[:, :NLT, 0, :] = c.transpose(1, 0, 2)
    tab[:, :NLT, 1, :] = s.transpose(1, 0, 2)
    pcon = np.zeros((P, 64), np.float32)
    pcon[:, 0:4] = [4, 3, 2, 1]
    pcon[:, 4:9] = [-1, 128, 256, 384, 512]
    pcon[:, 9:9 + LB] = np.arange(LB)
    pcon[:, 40] = np.arange(P) + 1
    pcon[:, 41:46] = np.arange(5) * 128
    pcon[:, 46:62] = 1.0
    return {
        "k_ident": np.eye(P, dtype=np.float32),
        "k_iota": np.tile(np.arange(P, dtype=np.float32), (P, 1)),
        "k_upper": np.triu(np.ones((P, P), np.float32), 1),
        "k_rope": tab,
        "k_pcon": pcon,
    }


_OUTS = [("y_prompt", (1, 128, 1024)), ("y_sample", (1, 512, 1024)),
         ("new_k", (1, 2, 128, 2, 64)), ("new_v", (1, 2, 128, 2, 64))]


def kernel(**inputs):
    import numpy as np
    import concourse.bacc as bacc
    from concourse.bass_utils import run_bass_kernel_spmd

    nc = bacc.Bacc("TRN2", target_bir_lowering=False, num_devices=1)
    arrays, I, O = {}, {}, {}
    for name, a in {**inputs, **shape_constants()}.items():
        a = np.ascontiguousarray(a)
        arrays[f"in_{name}"] = a
        I[name] = nc.dram_tensor(f"in_{name}", a.shape, mybir.dt.from_np(a.dtype), kind="ExternalInput").ap()
    for name, shape in _OUTS:
        O[name] = nc.dram_tensor(f"out_{name}", shape, F32, kind="ExternalOutput").ap()
    build(nc, I, O)
    r = run_bass_kernel_spmd(nc, [arrays], core_ids=[0])
    return tuple(r.results[0][f"out_{name}"] for name, _ in _OUTS)
```
